# Optimizing a Trainium2 kernel written in Bass

```python
import jax, jax.numpy as jnp
from jax import lax
import numpy as np

D_MODEL = 1024
BATCH = 1
SEQ = 512
DEPTH = 1

D_MIX = D_MODEL
D_ATTN = D_MIX // 2
D_CONV = D_MIX - D_ATTN
N_HEADS = 8
HEAD_DIM = D_ATTN // N_HEADS
CONV_WIDTH = 3
MOBA_BLOCK = 256
MOBA_TOPK = 3
Q_CHUNK = 64
ROPE_THETA = 10000.0
EPS = 1e-6
NEG = -1e30

kernel_name = "hymba_moba_shortconv_adaln_block"

def rmsnorm(x, g):
    xf = x.astype(jnp.float32)
    y = xf * lax.rsqrt(jnp.mean(xf * xf, axis=-1, keepdims=True) + EPS)
    return (y * g.astype(jnp.float32)).astype(x.dtype)

def rope(t, positions):
    half = HEAD_DIM // 2
    inv_freq = ROPE_THETA ** (-jnp.arange(half, dtype=jnp.float32) / half)
    ang = positions.astype(jnp.float32)[..., None] * inv_freq
    cos = jnp.cos(ang)[:, :, None, :]
    sin = jnp.sin(ang)[:, :, None, :]
    t1 = t[..., :half].astype(jnp.float32)
    t2 = t[..., half:].astype(jnp.float32)
    out = jnp.concatenate([t1 * cos - t2 * sin, t2 * cos + t1 * sin], axis=-1)
    return out.astype(t.dtype)

def moba_attention(q, k, v):
    B, H, S, Dh = q.shape
    nb = -(-S // MOBA_BLOCK)
    s_pad = nb * MOBA_BLOCK
    pad = [(0, 0), (0, 0), (0, s_pad - S), (0, 0)]
    q = jnp.pad(q, pad)
    k = jnp.pad(k, pad)
    v = jnp.pad(v, pad)
    kb = k.reshape(B, H, nb, MOBA_BLOCK, Dh)
    vb = v.reshape(B, H, nb, MOBA_BLOCK, Dh)
    scale = Dh ** -0.5
    n_sel = min(MOBA_TOPK, nb - 1)
    k_mean = jnp.mean(kb.astype(jnp.float32), axis=3)
    n_chunks = s_pad // Q_CHUNK
    q_chunks = q.reshape(B, H, n_chunks, Q_CHUNK, Dh).transpose(2, 0, 1, 3, 4)
    b_ix = jnp.arange(B)[:, None, None]
    h_ix = jnp.arange(H)[None, :, None]
    blk_ids = jnp.arange(nb)

    def chunk(args):
        ci, qc = args
        q_pos = ci * Q_CHUNK + jnp.arange(Q_CHUNK)
        own = (ci * Q_CHUNK) // MOBA_BLOCK
        k_own = lax.dynamic_index_in_dim(kb, own, axis=2, keepdims=False)
        v_own = lax.dynamic_index_in_dim(vb, own, axis=2, keepdims=False)
        k_pos = own * MOBA_BLOCK + jnp.arange(MOBA_BLOCK)
        logit_own = jnp.einsum('bhqd,bhld->bhql', qc, k_own,
                               preferred_element_type=jnp.float32) * scale
        logit_own = jnp.where(k_pos[None, :] <= q_pos[:, None], logit_own, NEG)
        if n_sel == 0:
            p_own = jax.nn.softmax(logit_own, axis=-1).astype(v.dtype)
            return jnp.einsum('bhql,bhld->bhqd', p_own, v_own)
        gate = jnp.einsum('bhqd,bhnd->bhqn', qc.astype(jnp.float32), k_mean)
        gate = jnp.where(blk_ids < own, gate, NEG)
        _, sel = lax.top_k(gate, n_sel)
        valid = sel < own
        sel_flat = sel.reshape(B, H, Q_CHUNK * n_sel)
        k_sel = kb[b_ix, h_ix, sel_flat].reshape(B, H, Q_CHUNK, n_sel, MOBA_BLOCK, Dh)
        v_sel = vb[b_ix, h_ix, sel_flat].reshape(B, H, Q_CHUNK, n_sel, MOBA_BLOCK, Dh)
        logit_past = jnp.einsum('bhqd,bhqnld->bhqnl', qc, k_sel,
                                preferred_element_type=jnp.float32) * scale
        logit_past = jnp.where(valid[..., None], logit_past, NEG)
        logit_past = logit_past.reshape(B, H, Q_CHUNK, n_sel * MOBA_BLOCK)
        logits = jnp.concatenate([logit_past, logit_own], axis=-1)
        p = jax.nn.softmax(logits, axis=-1).astype(v.dtype)
        p_past = p[..., :n_sel * MOBA_BLOCK].reshape(B, H, Q_CHUNK, n_sel, MOBA_BLOCK)
        p_own = p[..., n_sel * MOBA_BLOCK:]
        return (jnp.einsum('bhqnl,bhqnld->bhqd', p_past, v_sel)
                + jnp.einsum('bhql,bhld->bhqd', p_own, v_own))

    out = lax.map(chunk, (jnp.arange(n_chunks), q_chunks))
    out = out.transpose(1, 2, 0, 3, 4).reshape(B, H, s_pad, Dh)
    return out[:, :, :S]

def short_gated_conv(b_gate, c_gate, h, w_conv):
    u = c_gate * h
    y = lax.conv_general_dilated(
        u, w_conv[:, None, :], window_strides=(1,), padding=[(CONV_WIDTH - 1, 0)],
        dimension_numbers=('NWC', 'WIO', 'NWC'), feature_group_count=u.shape[-1])
    return b_gate * y

def setup_inputs(seed: int = 0) -> dict:
    key = jax.random.key(seed)
    ks = jax.random.split(key, 13)
    d_in_cols = 4 * D_ATTN + 4 * D_CONV
    x = jax.random.normal(ks[0], (BATCH, SEQ, D_MODEL), jnp.float32)
    c = jax.random.normal(ks[1], (BATCH, D_MODEL), jnp.float32)
    offsets = jax.random.randint(ks[2], (BATCH, 1), 0, 1024, dtype=jnp.int32)
    positions = jnp.arange(SEQ, dtype=jnp.int32)[None, :] + offsets
    w_ada = jax.random.normal(ks[3], (D_MODEL, 3 * D_MODEL), jnp.float32) * (0.5 * D_MODEL ** -0.5)
    b_ada = 0.01 * jax.random.normal(ks[4], (3 * D_MODEL,), jnp.float32)
    g_norm = 1.0 + 0.02 * jax.random.normal(ks[5], (D_MODEL,), jnp.float32)
    w_in = jax.random.normal(ks[6], (D_MODEL, d_in_cols), jnp.float32) * D_MODEL ** -0.5
    w_conv = jax.random.normal(ks[7], (CONV_WIDTH, D_CONV), jnp.float32) * CONV_WIDTH ** -0.5
    g_attn_out = 1.0 + 0.02 * jax.random.normal(ks[8], (D_ATTN,), jnp.float32)
    g_conv_out = 1.0 + 0.02 * jax.random.normal(ks[9], (D_CONV,), jnp.float32)
    w_out = jax.random.normal(ks[10], (D_MIX, D_MODEL), jnp.float32) * D_MIX ** -0.5
    g_final = 1.0 + 0.02 * jax.random.normal(ks[11], (D_MODEL,), jnp.float32)
    return {"x": x, "c": c, "positions": positions, "w_ada": w_ada, "b_ada": b_ada,
            "g_norm": g_norm, "w_in": w_in, "w_conv": w_conv, "g_attn_out": g_attn_out,
            "g_conv_out": g_conv_out, "w_out": w_out, "g_final": g_final}

def reference(x, c, positions, w_ada, b_ada, g_norm, w_in, w_conv, g_attn_out,
              g_conv_out, w_out, g_final):
    B, S, _ = x.shape
    splits = [D_ATTN, 2 * D_ATTN, 3 * D_ATTN, 4 * D_ATTN,
              4 * D_ATTN + D_CONV, 4 * D_ATTN + 2 * D_CONV, 4 * D_ATTN + 3 * D_CONV]
    for _ in range(DEPTH):
        mod = jax.nn.silu(c) @ w_ada + b_ada
        shift, scale, gate = jnp.split(mod, 3, axis=-1)
        h = rmsnorm(x, g_norm) * (1.0 + scale[:, None, :]) + shift[:, None, :]
        proj = h @ w_in
        q, k, v, z_attn, b_g, c_g, h_c, z_conv = jnp.split(proj, splits, axis=-1)
        q = rope(q.reshape(B, S, N_HEADS, HEAD_DIM), positions).transpose(0, 2, 1, 3)
        k = rope(k.reshape(B, S, N_HEADS, HEAD_DIM), positions).transpose(0, 2, 1, 3)
        v = v.reshape(B, S, N_HEADS, HEAD_DIM).transpose(0, 2, 1, 3)
        y_attn = moba_attention(q, k, v).transpose(0, 2, 1, 3).reshape(B, S, D_ATTN)
        y_attn = rmsnorm(y_attn, g_attn_out) * jax.nn.silu(z_attn)
        y_conv = short_gated_conv(b_g, c_g, h_c, w_conv)
        y_conv = rmsnorm(y_conv, g_conv_out) * jax.nn.silu(z_conv)
        y = jnp.concatenate([y_attn, y_conv], axis=-1) @ w_out
        x = x + gate[:, None, :] * y
    return rmsnorm(x, g_final)


_drawn_inputs = setup_inputs


def setup_inputs(seed=0):
    import zlib

    import numpy as np

    out = dict(_drawn_inputs(seed))
    spreads = {}
    factors = {'b_ada': 6.272, 'g_norm': 7.543, 'g_attn_out': 8.0, 'g_conv_out': 8.0, 'g_final': 2.824}
    for name, (base, spread) in spreads.items():
        noise = np.random.default_rng([zlib.crc32(name.encode()), seed]).standard_normal(out[name].shape)
        drawn = base * np.exp(spread * noise) if base else spread * noise
        out[name] = __import__('jax').numpy.asarray(drawn.astype(out[name].dtype))
    for name, factor in factors.items():
        out[name] = (out[name] * factor).astype(out[name].dtype)
    return out
```

```python
from contextlib import ExitStack

import concourse.bass as bass
from concourse import mybir

F32 = mybir.dt.float32
F32R = mybir.dt.float32r
I32 = mybir.dt.int32
ALU = mybir.AluOpType
ACT = mybir.ActivationFunctionType

P = 128
BANK = 512
HEAD_DIM = 64
CONV_TAPS = 3
EPS = 1e-6
MASKED = 1e30
PI = 3.141592653589793
TWO_PI_INV = 1.0 / (2.0 * PI)
ROUND = 1.5 * 2.0 ** 23
PI_BELOW = 3.1415925


def two_pi_pieces(bits, low):
    pieces, rest, unit = [], 2.0 * PI, 2.0 ** (3 - bits)
    while unit >= low:
        piece = int(rest / unit) * unit
        if piece:
            pieces.append(piece)
        rest -= piece
        unit /= 2.0 ** bits
    return pieces


def build(nc, x, c, positions, w_ada, b_ada, g_norm, w_in, w_conv, g_attn_out, g_conv_out,
          w_out, g_final, inv_freq, out):
    _, S, D = x.shape
    DA = g_attn_out.shape[0]
    KT = D // P
    TT = S // P
    NP = DA // P
    HALF = HEAD_DIM // 2
    R = D // P
    RV = 6
    assert S == BANK and KT == 8 and TT == 4 and NP == 4 and D == 2 * BANK

    C_, H_, B_, ZC, ZA = range(5)
    COLS = [5 * DA, 6 * DA, 4 * DA, 7 * DA, 3 * DA]
    NT = len(COLS)
    TILE_BANK = [0, 1, 0, 1, 0]
    RAW_SLOT = [0, 1, 2, 0, 1]

    S_AT = {3: 0, 2: 512, 0: 896, 1: 1024}
    T_AT = {0: 0, 1: 512, 3: 896, 2: 1024}
    S_ORDER = [2, 0, 3, 1]
    TRI = 1280
    SB, TB = 2 * BANK, 5 * BANK

    with ExitStack() as ctx:
        cursor = [(nc.sbuf_base + 31) // 32 * 32]

        def at(name, offset, shape, dt=F32):
            return nc.alloc_sbuf_tensor_at(name, [P, *shape], dt, offset=offset)

        def sb(name, shape, dt=F32):
            size = 4
            for n in shape:
                size *= n
            offset = cursor[0]
            cursor[0] = (offset + size + 31) // 32 * 32
            return at(name, offset, shape, dt)

        def sem(name):
            return ctx.enter_context(nc.semaphore(name))

        h_hi = sb("h_hi", [KT, S], F32R)
        h_lo = sb("h_lo", [KT, S], F32R)
        w_hi = sb("w_hi", [8, BANK], F32R)
        w_lo = sb("w_lo", [8, BANK], F32R)
        w_raw = sb("w_raw", [4, BANK])
        tile_raw = sb("tile_raw", [3, KT, P])
        rope_q = sb("rope_q", [TT, P])
        rope_k = sb("rope_k", [TT, P])
        cos_t = sb("cos_t", [TT, HEAD_DIM])
        sin_t = sb("sin_t", [TT, HEAD_DIM])
        qs = sb("qs", [2, S], F32R)
        k_hi = sb("k_hi", [2, S], F32R)
        k_lo = sb("k_lo", [2, S], F32R)
        pt_hi = sb("pt_hi", [TRI], F32R)
        pt_lo = sb("pt_lo", [TRI], F32R)
        v2 = sb("v2", [2, TT, P], F32R)
        cz = sb("cz", [S])
        u = sb("u", [S + CONV_TAPS - 1])
        yc = sb("yc", [S])
        yg = sb("yg", [S])
        ytmp = sb("ytmp", [S])
        ya = sb("ya", [S])
        za = sb("za", [S])
        sq = sb("sq", [S])
        sqsum = sb("sqsum", [2, S])
        mask = sb("mask", [S])
        ident = sb("ident", [P])
        ones = sb("ones", [P])
        gate = sb("gate", [D])
        prmT = sb("prmT", [64])
        cs = sb("cs", [R])
        sc = sb("sc", [R])
        gs = sb("gs", [KT])
        sh = sb("sh", [KT])
        b1 = sb("b1", [KT])
        small = sb("small", [64])
        rmin = sb("rmin", [8])
        psums = sb("psums", [8])
        prec = sb("prec", [8])
        rs = sb("rs", [8])
        ss2 = sb("ss2", [8])
        posT = sb("posT", [TT])
        base = cursor[0]
        sb("probs_", [TRI])
        probs = at("probs", base, [TRI])
        rope_m = at("rope_m", base, [2, TT, P])
        base = cursor[0]
        sb("y_", [NP, 4, S])
        xt = at("xt", base, [TT, D])
        qkv = at("qkv", base, [NP, 4, S])
        y = at("y", base, [NP, 4, S], F32R)
        base = cursor[0]
        sb("tile_", [2 * NT, KT * P])
        t_hi = at("t_hi", base, [NT, KT, P], F32R)
        t_lo = at("t_lo", base + NT * KT * P * 4, [NT, KT, P], F32R)
        ada = at("ada", base, [3, 2, R, P])
        acc = at("acc", base + 24576, [2, 2, P])
        prod = at("prod", base + 26624, [2, 2, 2, P])
        h32 = at("h32", base + 30720, [2, S])
        junk = at("junk", base + 34816, [D])
        x2 = at("x2", base, [TT, D])
        gfin = at("gfin", base + 16384, [D])
        oc = at("oc", base + 20480, [TT, BANK])
        om = at("om", base + 28672, [2, BANK])
        junk2 = at("junk2", base + 32768, [BANK])
        prm = at("prm", base + 38912, [P])
        posi = at("posi", base + 39424, [P], I32)
        posf = at("posf", base + 39936, [P])
        invf = sb("invf", [HALF])
        ang = sb("ang", [TT, HALF])
        turns = sb("turns", [TT, HALF])
        assert cursor[0] <= nc.sbuf_usable_end, (cursor[0], nc.sbuf_usable_end)

        ps = ctx.enter_context(nc.psum_tensor("ps", [P, 8 * BANK], F32))

        def bank(b, lo=0, hi=BANK, p0=0, p1=P):
            return ps[p0:p1, b * BANK + lo:b * BANK + hi]

        c_in, pos_in, prm_in, gate_in = sem("c_in"), sem("pos_in"), sem("prm_in"), sem("gate_in")
        x_in = [sem(f"x_in{m}") for m in range(TT)]
        ada_in = [sem(f"ada_in{i}") for i in range(3)]
        raw_in = [sem(f"raw_in{i}") for i in range(4)]
        tile_in = [sem(f"tile_in{i}") for i in range(3)]
        x2_in, gfin_in, out_done = sem("x2_in"), sem("gfin_in"), sem("out_done")
        ident_ok, mask_ok, ones_ok, pool_step = sem("ident_ok"), sem("mask_ok"), sem("ones_ok"), sem("pool_step")
        silu_c, x_sq, x_rstd, x_norm = sem("silu_c"), sem("x_sq"), sem("x_rstd"), sem("x_norm")
        prm_tr, pos_tr, prm_ok, posf_ok = sem("prm_tr"), sem("pos_tr"), sem("prm_ok"), sem("posf_ok")
        chain, prods, mod_sum, mod_ok = sem("chain"), sem("prods"), sem("mod_sum"), sem("mod_ok")
        x_tr, h_ok, hhi_ok, hlo_ok = sem("x_tr"), sem("h_ok"), sem("hhi_ok"), sem("hlo_ok")
        slab_hi, slab_lo, slab_used = sem("slab_hi"), sem("slab_lo"), sem("slab_used")
        qkv_out, qkv_evac, gate_sum, gate_ok = sem("qkv_out"), sem("qkv_evac"), sem("gate_sum"), sem("gate_ok")
        dve_step, angle_ok, trig_ok, rope_ok = sem("dve_step"), sem("angle_ok"), sem("trig_ok"), sem("rope_ok")
        tile_hi, tile_lo, tile_out = sem("tile_hi"), sem("tile_lo"), sem("tile_out")
        bank0_free, bank1_free, u_ok, tap_ok = sem("bank0_free"), sem("bank1_free"), sem("u_ok"), sem("tap_ok")
        qk_tr, qk_hi, qk_split, v_hi, v_lo = sem("qk_tr"), sem("qk_hi"), sem("qk_split"), sem("v_hi"), sem("v_lo")
        scores, row_min, exps, p_norm = sem("scores"), sem("row_min"), sem("exps"), sem("p_norm")
        p_tr, p_hi, p_lo, pv_out = sem("p_tr"), sem("p_hi"), sem("p_lo"), sem("pv_out")
        y_tmp, y_attn, c_copy, y_conv = sem("y_tmp"), sem("y_attn"), sem("c_copy"), sem("y_conv")
        y_gated, y_hi, y_lo = sem("y_gated"), sem("y_hi"), sem("y_lo")
        sq_ok, sq_added = sem("sq_ok"), sem("sq_added")
        ssq_out, ssq_ok, rs_ok = sem("ssq_out"), sem("ssq_ok"), sem("rs_ok")
        conv_out, attn_out, conv_evac, attn_evac = sem("conv_out"), sem("attn_out"), sem("conv_evac"), sem("attn_evac")
        x2_ok, x2_sq, fin_ss, fin_rs, fin_ok = sem("x2_ok"), sem("x2_sq"), sem("fin_ss"), sem("fin_rs"), sem("fin_ok")

        w_ada_v = w_ada.rearrange("(p r) n -> p r n", r=R)
        w_in_v = w_in.rearrange("(k p) n -> k p n", p=P)
        w_in_t = w_in.rearrange("(k p) n -> p k n", p=P)
        w_out_v = w_out.rearrange("(k p) n -> k p n", p=P)
        pair_raw = lambda t, part: t[:, :, part, :]

        block = ctx.enter_context(nc.Block())

        @block.sync
        def _(sp):
            sp.dma_start(cs[:, :], c.rearrange("a (p r) -> p (a r)", r=R)).then_inc(c_in, 16)
            for m in range(TT):
                sp.dma_start(xt[:, m, :], x[0, m * P:(m + 1) * P, :]).then_inc(x_in[m], 16)
            for j in range(KT):
                if j == 1:
                    row = 0
                    for src in (b_ada.rearrange("(t p) -> t p", p=P), g_norm.rearrange("(t p) -> t p", p=P),
                                g_attn_out.rearrange("(t p) -> t p", p=P), g_conv_out.rearrange("(t p) -> t p", p=P),
                                w_conv.rearrange("a (t p) -> (a t) p", p=P)):
                        n = src.shape[0]
                        sp.dma_start(prm[row:row + n, :], src).then_inc(prm_in, 16)
                        row += n
                if j >= 3:
                    sp.wait_ge(chain, RV * (j - 2))
                    sp.wait_ge(prods, 2 * (j - 2))
                for two in range(2):
                    col = (1 - two) * D + j * P
                    sp.dma_start(ada[:, j % 3, two], w_ada_v[:, :, col:col + P]).then_inc(ada_in[j % 3], 16)
                if j >= 4:
                    sp.wait_ge(slab_lo, j - 3)
                sp.dma_start(w_raw[:, j % 4], w_in_v[j, :, 0:BANK]).then_inc(raw_in[j % 4], 16)
                if j == 1:
                    sp.dma_start(posi[0:TT, :], positions.rearrange("a (t p) -> (a t) p", p=P)).then_inc(pos_in, 16)
                    sp.dma_start(invf[:, :], inv_freq.partition_broadcast(P)).then_inc(pos_in, 16)
            sp.dma_start(gate[:, :], b_ada[2 * D:3 * D].partition_broadcast(P)).then_inc(gate_in, 16)
            with sp.Fori(1, 3) as g:
                for k in range(KT):
                    if k in (2, 5):
                        i = k // 3
                        sp.wait_ge(chain, RV * KT + R * (2 * g - 2))
                        sp.wait_ge(prods, 2 * KT)
                        for two in range(2):
                            sp.dma_start(ada[:, i, two],
                                         w_ada_v[:, :, bass.ds(g * (2 * 256) + (2 * D - 512 + i * 256 + two * P), P)]
                                         ).then_inc(ada_in[i], 16)
                    sp.wait_ge(slab_lo, 8 * g + (k - 3))
                    sp.dma_start(w_raw[:, k % 4], w_in_v[k, :, bass.ds(g * BANK, BANK)]).then_inc(raw_in[k % 4], 16)
            for t in (C_, H_):
                sp.dma_start(tile_raw[:, RAW_SLOT[t]], w_in_t[:, :, COLS[t]:COLS[t] + P]
                             ).then_inc(tile_in[RAW_SLOT[t]], 16)

            def turn(p, last):
                todo = [(B_, 0, 1), (ZC, 0, 1), (ZA, 0, 2)] + ([] if last else [(C_, 1, 4), (H_, 1, 5)])
                for t, ahead, split in todo:
                    sp.wait_ge(tile_lo, p * NT + split)
                    sp.dma_start(tile_raw[:, RAW_SLOT[t]],
                                 w_in_t[:, :, bass.ds(p * P + (COLS[t] + ahead * P), P)]
                                 ).then_inc(tile_in[RAW_SLOT[t]], 16)
                    if t in (B_, ZA):
                        i = int(t == ZA)
                        sp.wait_ge(slab_lo, p * 2 + 3 * KT)
                        sp.dma_start(w_raw[:, i], w_out_v[bass.ds(p * 2 + i, 1), :, 0:BANK].rearrange("a p n -> p (a n)")
                                     ).then_inc(raw_in[i], 16)

            with sp.Fori(0, NP - 1) as p:
                turn(p, False)
            turn(NP - 1, True)
            sp.wait_ge(slab_lo, 4 * KT)
            for k in (4, 5, 6, 7):
                sp.dma_start(w_raw[:, k % 4], w_out_v[k, :, BANK:D]).then_inc(raw_in[k % 4], 16)
            sp.wait_ge(tile_out, NT * NP)
            for m in range(TT):
                sp.dma_start(x2[:, m, :], x[0, m * P:(m + 1) * P, :]).then_inc(x2_in, 16)
            sp.dma_start(gfin[:, :], g_final.partition_broadcast(P)).then_inc(gfin_in, 16)
            for k in (0, 1, 2, 3):
                sp.wait_ge(slab_lo, 4 * KT + k + 1)
                sp.dma_start(w_raw[:, k % 4], w_out_v[k, :, BANK:D]).then_inc(raw_in[k % 4], 16)
            for m in range(TT):
                sp.wait_ge(fin_ok, m + 1)
                sp.dma_start(out[0, m * P:(m + 1) * P, :], x2[:, m, :]).then_inc(out_done, 16)
            sp.wait_ge(out_done, 16 * TT)

        @block.scalar
        def _(act):
            act.wait_ge(c_in, 16)
            nc.scalar.activation(sc[:, :], cs[:, :], ACT.Silu).then_inc(silu_c, 1)
            for m in range(TT):
                act.wait_ge(x_in[m], 16)
                if m:
                    act.wait_ge(x_sq, m)
                nc.scalar.activation(junk[:, :], xt[:, m, :], ACT.Square,
                                     accum_out=small[:, m:m + 1]).then_inc(x_sq, 1)
            act.wait_ge(silu_c, 1)

            def slab(k, raw_turn, count):
                act.wait_ge(raw_in[k % 4], raw_turn)
                nc.scalar.activation(w_hi[:, k], w_raw[:, k % 4], ACT.Copy).then_inc(slab_hi, 1)

            def products(j):
                act.wait_ge(ada_in[j % 3], 32 * (j // 3 + 1))
                if j >= 2:
                    act.wait_ge(mod_sum, j - 1)
                for i in range(R - RV):
                    nc.scalar.activation(prod[:, j % 2, i], ada[:, j % 3, :, RV + i, :], ACT.Copy,
                                         scale=sc[:, RV + i:RV + i + 1]).then_inc(prods, 1)

            def split_h(j):
                act.wait_ge(h_ok, j + 1)
                nc.scalar.activation(h_hi[:, j], h32[:, j % 2], ACT.Copy).then_inc(hhi_ok, 1)

            products(0)
            for j in range(KT):
                slab(j, 16 * (j // 4 + 1), 0)
                if j + 1 < KT:
                    products(j + 1)
                split_h(j)

            act.wait_ge(angle_ok, 1)
            sin_v = sin_t.rearrange("p m (two f) -> p m two f", two=2)
            cos_v = cos_t.rearrange("p m (two f) -> p m two f", two=2)
            for two in range(2):
                nc.scalar.activation(sin_v[:, :, two, :], ang[:, :, :], ACT.Sin).then_inc(trig_ok, 1)
                nc.scalar.activation(cos_v[:, :, two, :], turns[:, :, :], ACT.Sin).then_inc(trig_ok, 1)

            def evacuate(g, m):
                act.wait_ge(x_sq, TT)
                act.wait_ge(qkv_out, g * TT + (m + 1))
                out_ap = qkv[:, :, g, m * P:(m + 1) * P] if isinstance(g, int) else \
                    qkv[:, :, bass.ds(g, 1), m * P:(m + 1) * P].rearrange("p a g n -> p a (g n)")
                ins = nc.scalar.activation(out_ap, bank(m).rearrange("p (a n) -> p a n", n=P), ACT.Copy)
                ins.then_inc(qkv_evac, 1)

            with act.Fori(1, 3) as g:
                for k in range(KT):
                    if k < KT - 1:
                        act.wait_ge(slab_used, g * (KT - 1) + (k + 1 - (KT - 1)))
                    else:
                        for m in range(TT):
                            evacuate(g - 1, m)
                    act.wait_ge(raw_in[k % 4], g * 32 + 16 * (k // 4 + 1))
                    nc.scalar.activation(w_hi[:, k], w_raw[:, k % 4], ACT.Copy).then_inc(slab_hi, 1)
            act.wait_ge(chain, RV * KT + 4 * R)
            act.wait_ge(gate_sum, 4)

            def split_tile(t, arrived):
                act.wait_ge(tile_in[RAW_SLOT[t]], arrived)
                nc.scalar.activation(t_hi[:, t], tile_raw[:, RAW_SLOT[t]], ACT.Copy).then_inc(tile_hi, 1)

            split_tile(C_, 16)
            split_tile(H_, 16)
            for m in range(TT):
                act.wait_ge(qkv_out, 2 * TT + m + 1)
                ins = nc.scalar.activation(qkv[:, :, 2, m * P:(m + 1) * P],
                                           bank(m).rearrange("p (a n) -> p a n", n=P), ACT.Copy)
                ins.then_inc((bank0_free, bank1_free, qkv_evac, qkv_evac)[m], 1)
            act.wait_ge(bank0_free, 1)
            act.wait_ge(bank1_free, 1)
            act.wait_ge(qkv_evac, 2 * TT + 2)

            def exponents(p, head):
                for n, i in enumerate(S_ORDER):
                    act.wait_ge(row_min, p * 8 + (4 * head + n + 1))
                    a, w = S_AT[i], P * (i + 1)
                    e = 4 * head + n
                    nc.scalar.activation(probs[:, a:a + w], probs[:, a:a + w], ACT.Exp, scale=-1.0,
                                         bias=rmin[:, e:e + 1], accum_out=psums[:, e:e + 1]).then_inc(exps, 1)

            def turn(p, last):
                for head in range(2):
                    hc = head * HEAD_DIM
                    src = qkv[:, p, 2, :] if last else qkv[:, bass.ds(p, 1), 2, :].rearrange("p a n -> p (a n)")
                    nc.scalar.activation(v2[:, head, :, hc:hc + HEAD_DIM],
                                         src.rearrange("p (m n) -> p m n", n=P)[:, :, hc:hc + HEAD_DIM],
                                         ACT.Copy).then_inc(v_hi, 1)
                act.wait_ge(tile_out, p * NT + (C_ + 1))
                nc.scalar.activation(cz[:, :], bank(0), ACT.Copy).then_inc(c_copy, 1)
                act.wait_ge(qk_tr, p * 2 + 1)
                for head in range(2):
                    a, b = head * 64, head * 64 + 64
                    nc.scalar.activation(qs[a:b, head, :], bank(5, p0=a, p1=b), ACT.Copy,
                                         scale=-(HEAD_DIM ** -0.5)).then_inc(qk_hi, 1)
                act.wait_ge(qk_tr, p * 2 + 2)
                for head in range(2):
                    a, b = head * 64, head * 64 + 64
                    for to in range(2):
                        nc.scalar.activation(k_hi[to * 64:to * 64 + 64, head, :], bank(6, p0=a, p1=b),
                                             ACT.Copy).then_inc(qk_hi, 1)
                split_tile(B_, p * 16 + 16)
                split_tile(ZC, p * 32 + 32)
                exponents(p, 0)
                act.wait_ge(p_tr, p * 2 + 1)
                nc.scalar.activation(pt_hi[:, :], ps[:, TB:TB + TRI], ACT.Copy).then_inc(p_hi, 1)
                exponents(p, 1)
                split_tile(ZA, p * 32 + 32)
                act.wait_ge(y_conv, p + 1)
                act.wait_ge(sq_added, p * 2 + 1)
                nc.scalar.activation(sq[:, :], yc[:, :], ACT.Square).then_inc(sq_ok, 1)
                act.wait_ge(pv_out, p * 2 + 1)
                nc.scalar.activation(ytmp[0:64, :], bank(2, p0=64, p1=128), ACT.Copy).then_inc(y_tmp, 1)
                act.wait_ge(p_tr, p * 2 + 2)
                nc.scalar.activation(pt_hi[:, :], ps[:, TB:TB + TRI], ACT.Copy).then_inc(p_hi, 1)
                act.wait_ge(tile_out, p * NT + (ZC + 1))
                nc.scalar.activation(cz[:, :], bank(1), ACT.Silu).then_inc(bank1_free, 1)
                if not last:
                    split_tile(C_, p * 32 + 48)
                for i in range(2):
                    act.wait_ge(qkv_out, 3 * TT)
                    act.wait_ge(raw_in[i], p * 16 + (16 * 6 + 16))
                    nc.scalar.activation(w_hi[:, bass.ds(p * 2 + i, 1)].rearrange("p a n -> p (a n)"),
                                         w_raw[:, i], ACT.Copy).then_inc(slab_hi, 1)
                act.wait_ge(qkv_evac, 2 * TT + 2)
                act.wait_ge(y_gated, p * 2 + 1)
                yp = y[:, p] if last else y[:, bass.ds(p, 1)].rearrange("p a s n -> p (a s) n")
                nc.scalar.activation(yp[:, 2], yg[:, :], ACT.Copy).then_inc(y_hi, 1)
                if not last:
                    split_tile(H_, p * 32 + 48)
                act.wait_ge(tile_out, p * NT + (ZA + 1))
                nc.scalar.activation(za[:, :], bank(0), ACT.Silu).then_inc(bank0_free, 1)
                act.wait_ge(pv_out, p * 2 + 2)
                nc.scalar.activation(ytmp[64:128, :], bank(3, p0=0, p1=64), ACT.Copy).then_inc(y_tmp, 1)
                act.wait_ge(y_attn, p * 2 + 2)
                act.wait_ge(sq_added, p * 2 + 2)
                nc.scalar.activation(sq[:, :], ya[:, :], ACT.Square).then_inc(sq_ok, 1)
                act.wait_ge(qkv_evac, 2 * TT + 2)
                act.wait_ge(y_gated, p * 2 + 2)
                nc.scalar.activation(yp[:, 0], yg[:, :], ACT.Copy).then_inc(y_hi, 1)

            with act.Fori(0, NP - 1) as p:
                turn(p, False)
            turn(NP - 1, True)

            act.wait_ge(conv_out, TT)
            for k in (4, 5, 6, 7):
                act.wait_ge(raw_in[k % 4], 16 * (7 + (4 if k % 4 < 2 else 0)))
                nc.scalar.activation(w_hi[:, k], w_raw[:, k % 4], ACT.Copy).then_inc(slab_hi, 1)
            act.wait_ge(rs_ok, 1)
            act.wait_ge(x2_in, 16 * TT)
            for n in range(2):
                for m in range(TT):
                    if n:
                        act.wait_ge(attn_evac, m + 1)
                    act.wait_ge(conv_out, n * TT + m + 1)
                    nc.scalar.activation(oc[:, m], bank(m), ACT.Copy, scale=rs[:, m:m + 1]).then_inc(conv_evac, 1)
                if n == 0:
                    act.wait_ge(attn_out, TT)
                    for k in (0, 1, 2, 3):
                        act.wait_ge(raw_in[k % 4], 16 * (8 + (4 if k % 4 < 2 else 0)))
                        nc.scalar.activation(w_hi[:, k], w_raw[:, k % 4], ACT.Copy).then_inc(slab_hi, 1)
                for m in range(TT):
                    act.wait_ge(x2_ok, n * TT + m + 1)
                    if n or m:
                        act.wait_ge(x2_sq, n * TT + m)
                    nc.scalar.activation(junk2[:, :], x2[:, m, n * BANK:(n + 1) * BANK], ACT.Square,
                                         accum_out=ss2[:, n * TT + m:n * TT + m + 1]).then_inc(x2_sq, 1)

        @block.gpsimd
        def _(pool):
            nc.gpsimd.memset(ident[:, :], 0.0).then_inc(pool_step, 1)
            nc.gpsimd.memset(mask[:, :], 0.0).then_inc(pool_step, 1)
            nc.gpsimd.memset(small[:, 32:40], -0.5).then_inc(pool_step, 1)
            nc.gpsimd.memset(sqsum[:, :, :], 0.0).then_inc(sq_added, 1)
            pool.wait_ge(pool_step, 1)
            nc.gpsimd.affine_select(out=ident[:, :], in_=ident[:, :], compare_op=ALU.not_equal, fill=1.0, base=0,
                                    pattern=[[-1, P]], channel_multiplier=1).then_inc(ident_ok, 1)
            pool.wait_ge(pool_step, 2)
            nc.gpsimd.affine_select(out=mask[:, S - P:S], in_=mask[:, S - P:S], compare_op=ALU.is_ge, fill=MASKED,
                                    base=0, pattern=[[-1, P]], channel_multiplier=1).then_inc(mask_ok, 1)
            pool.wait_ge(x_sq, TT)
            nc.gpsimd.tensor_scalar(small[:, 8:8 + TT], small[:, 0:TT], 1.0 / D, EPS, ALU.mult, ALU.add
                                    ).then_inc(pool_step, 1)
            pool.wait_ge(pool_step, 4)
            nc.gpsimd.tensor_tensor(small[:, 16:16 + TT], small[:, 8:8 + TT], small[:, 32:32 + TT], ALU.pow
                                    ).then_inc(x_rstd, 1)

            for j in range(KT):
                pool.wait_ge(slab_hi, j + 1)
                nc.gpsimd.tensor_tensor(w_lo[:, j], w_raw[:, j % 4], w_hi[:, j].bitcast(F32), ALU.subtract
                                        ).then_inc(slab_lo, 1)
                pool.wait_ge(hhi_ok, j + 1)
                nc.gpsimd.tensor_tensor(h_lo[:, j], h32[:, j % 2], h_hi[:, j].bitcast(F32), ALU.subtract
                                        ).then_inc(hlo_ok, 1)
            with pool.Fori(1, 3) as g:
                for k in range(KT):
                    pool.wait_ge(slab_hi, g * KT + (k + 1))
                    nc.gpsimd.tensor_tensor(w_lo[:, k], w_raw[:, k % 4], w_hi[:, k].bitcast(F32), ALU.subtract
                                            ).then_inc(slab_lo, 1)

            def split_tile(t, count):
                pool.wait_ge(tile_hi, count)
                nc.gpsimd.tensor_tensor(t_lo[:, t], tile_raw[:, RAW_SLOT[t]], t_hi[:, t].bitcast(F32), ALU.subtract
                                        ).then_inc(tile_lo, 1)

            split_tile(C_, 1)
            split_tile(H_, 2)

            def turn(p, last):
                for head in range(2):
                    pool.wait_ge(v_hi, p * 2 + (head + 1))
                    hc, lc = head * HEAD_DIM, (1 - head) * HEAD_DIM
                    src = qkv[:, p, 2, :] if last else qkv[:, bass.ds(p, 1), 2, :].rearrange("p a n -> p (a n)")
                    nc.gpsimd.tensor_tensor(v2[:, head, :, lc:lc + HEAD_DIM],
                                            src.rearrange("p (m n) -> p m n", n=P)[:, :, hc:hc + HEAD_DIM],
                                            v2[:, head, :, hc:hc + HEAD_DIM].bitcast(F32), ALU.subtract
                                            ).then_inc(v_lo, 1)
                split_tile(B_, p * NT + 3)
                split_tile(ZC, p * NT + 4)
                split_tile(ZA, p * NT + 5)
                pool.wait_ge(sq_ok, p * 2 + 1)
                pool.wait_ge(sq_added, p * 2 + 1)
                nc.gpsimd.tensor_tensor(sqsum[:, 0], sqsum[:, 0], sq[:, :], ALU.add).then_inc(sq_added, 1)
                if not last:
                    split_tile(C_, p * NT + 6)
                for i in range(2):
                    pool.wait_ge(slab_hi, p * 2 + (3 * KT + i + 1))
                    s = bass.ds(p * 2 + i, 1)
                    nc.gpsimd.tensor_tensor(w_lo[:, s].rearrange("p a n -> p (a n)"), w_raw[:, i],
                                            w_hi[:, s].rearrange("p a n -> p (a n)").bitcast(F32), ALU.subtract
                                            ).then_inc(slab_lo, 1)
                yp = y[:, p] if last else y[:, bass.ds(p, 1)].rearrange("p a s n -> p (a s) n")
                pool.wait_ge(y_hi, p * 2 + 1)
                nc.gpsimd.tensor_tensor(yp[:, 3], yg[:, :], yp[:, 2].bitcast(F32), ALU.subtract).then_inc(y_lo, 1)
                if not last:
                    split_tile(H_, p * NT + 7)
                pool.wait_ge(sq_ok, p * 2 + 2)
                nc.gpsimd.tensor_tensor(sqsum[:, 1], sqsum[:, 1], sq[:, :], ALU.add).then_inc(sq_added, 1)
                pool.wait_ge(y_hi, p * 2 + 2)
                nc.gpsimd.tensor_tensor(yp[:, 1], yg[:, :], yp[:, 0].bitcast(F32), ALU.subtract).then_inc(y_lo, 1)

            with pool.Fori(0, NP - 1) as p:
                turn(p, False)
            turn(NP - 1, True)
            pool.wait_ge(slab_hi, 4 * KT + 4)
            for k in (4, 5, 6, 7):
                nc.gpsimd.tensor_tensor(w_lo[:, k], w_raw[:, k % 4], w_hi[:, k].bitcast(F32), ALU.subtract
                                        ).then_inc(slab_lo, 1)
            pool.wait_ge(ssq_ok, 1)
            nc.gpsimd.tensor_tensor(rs[:, :], small[:, 40:48], small[:, 32:40], ALU.pow).then_inc(rs_ok, 1)
            for k in (0, 1, 2, 3):
                pool.wait_ge(slab_hi, 4 * KT + 4 + k + 1)
                nc.gpsimd.tensor_tensor(w_lo[:, k], w_raw[:, k % 4], w_hi[:, k].bitcast(F32), ALU.subtract
                                        ).then_inc(slab_lo, 1)
            for m in range(TT):
                pool.wait_ge(fin_ss, m + 1)
                nc.gpsimd.tensor_tensor(small[:, 56 + m:57 + m], small[:, 48 + m:49 + m], small[:, 32:33], ALU.pow
                                        ).then_inc(fin_rs, 1)

        @block.vector
        def _(dve):
            steps = [0]

            def step(ins):
                ins.then_inc(dve_step, 1)
                steps[0] += 1
                dve.wait_ge(dve_step, steps[0])

            nc.vector.memset(ones[:, :], 1.0).then_inc(ones_ok, 1)
            nc.vector.memset(u[:, 0:CONV_TAPS - 1], 0.0).then_inc(ones_ok, 1)

            def sum_chunk(j, buf, n, arrived, start):
                dve.wait_ge(ada_in[buf], arrived)
                for r in range(n):
                    src = ada[:, buf, :, r, :]
                    if r == 0:
                        ins = nc.vector.tensor_scalar(acc[:, j % 2], src, sc[:, 0:1], None, ALU.mult)
                    else:
                        dve.wait_ge(chain, start + r)
                        ins = nc.vector.scalar_tensor_tensor(out=acc[:, j % 2], in0=src, scalar=sc[:, r:r + 1],
                                                             in1=acc[:, j % 2], op0=ALU.mult, op1=ALU.add)
                    ins.then_inc(chain, 1)

            def modulation(j):
                dve.wait_ge(mod_sum, j + 1)
                b = 6 + j % 2
                nc.vector.tensor_scalar(gs[:, j:j + 1], bank(b, 0, 1), b1[:, j:j + 1], prmT[:, 24 + j:25 + j],
                                        ALU.add, ALU.mult).then_inc(mod_ok, 1)
                nc.vector.tensor_scalar(sh[:, j:j + 1], bank(b, 1, 2), prmT[:, j:j + 1], None,
                                        ALU.add).then_inc(mod_ok, 1)
                dve.wait_ge(mod_ok, 2 * j + 2)
                dve.wait_ge(x_tr, j + 1)
                if j >= 2:
                    dve.wait_ge(hlo_ok, j - 1)
                nc.vector.tensor_scalar(h32[:, j % 2], bank(4 + j % 2), gs[:, j:j + 1], sh[:, j:j + 1],
                                        ALU.mult, ALU.add).then_inc(h_ok, 1)

            dve.wait_ge(silu_c, 1)
            sum_chunk(0, 0, RV, 32, 0)
            dve.wait_ge(x_rstd, 1)
            for m in range(TT):
                nc.vector.tensor_scalar(xt[:, m, :], xt[:, m, :], small[:, 16 + m:17 + m], None,
                                        ALU.mult).then_inc(x_norm, 1)
            dve.wait_ge(prm_tr, 1)
            step(nc.vector.tensor_copy(prmT[:, 0:52], bank(6, 0, 52)))
            nc.vector.tensor_scalar(b1[:, :], prmT[:, 8:16], 1.0, None, ALU.add).then_inc(prm_ok, 1)
            dve.wait_ge(prm_ok, 1)
            for j in range(KT):
                if j + 1 < KT:
                    if j + 1 >= 2:
                        dve.wait_ge(mod_sum, j)
                    sum_chunk(j + 1, (j + 1) % 3, RV, 32 * ((j + 1) // 3 + 1), RV * (j + 1))
                modulation(j)

            dve.wait_ge(pos_in, 32)
            nc.vector.tensor_copy(posf[0:TT, :], posi[0:TT, :]).then_inc(posf_ok, 1)
            dve.wait_ge(pos_tr, 1)
            step(nc.vector.tensor_copy(posT[:, :], bank(6, 0, TT)))
            for m in range(TT):
                ins = nc.vector.tensor_scalar(ang[:, m, :], invf[:, :], posT[:, m:m + 1], None, ALU.mult)
            step(ins)
            step(nc.vector.tensor_scalar(turns[:, :, :], ang[:, :, :], TWO_PI_INV, ROUND, ALU.mult, ALU.add))
            step(nc.vector.tensor_scalar(turns[:, :, :], turns[:, :, :], ROUND, None, ALU.subtract))
            for piece in two_pi_pieces(4, 2.0 ** -45):
                step(nc.vector.scalar_tensor_tensor(out=ang[:, :, :], in0=turns[:, :, :], scalar=-piece,
                                                    in1=ang[:, :, :], op0=ALU.mult, op1=ALU.add))
            step(nc.vector.tensor_scalar(ang[:, :, :], ang[:, :, :], PI_BELOW, -PI_BELOW, ALU.min, ALU.max))
            step(nc.vector.scalar_tensor_tensor(out=turns[:, :, :], in0=ang[:, :, :], scalar=-1.0, in1=ang[:, :, :],
                                                op0=ALU.mult, op1=ALU.min))
            nc.vector.tensor_scalar(turns[:, :, :], turns[:, :, :], PI / 2, None, ALU.add).then_inc(angle_ok, 1)

            dve.wait_ge(gate_in, 16)
            dve.wait_ge(mod_sum, KT)
            with dve.Fori(1, 3) as g:
                for i in range(2):
                    dve.wait_ge(ada_in[i], g * 32 + 32 * 3)
                    for r in range(R):
                        src = ada[:, i, :, r, :]
                        if r == 0:
                            ins = nc.vector.tensor_scalar(acc[:, i], src, sc[:, 0:1], None, ALU.mult)
                        else:
                            dve.wait_ge(chain, g * (2 * R) + (RV * KT - 2 * R + i * R + r))
                            ins = nc.vector.scalar_tensor_tensor(out=acc[:, i], in0=src, scalar=sc[:, r:r + 1],
                                                                 in1=acc[:, i], op0=ALU.mult, op1=ALU.add)
                        ins.then_inc(chain, 1)
                for i in range(2):
                    dve.wait_ge(gate_sum, g * 2 + (i - 1))
                    gg = gate[:, bass.ds(g * 512 + (i * 256 - 512), 256)]
                    nc.vector.tensor_tensor(gg, gg, bank(4 + i, 0, 256), ALU.add).then_inc(gate_ok, 1)

            def rope_part(p, part, to, count):
                if isinstance(p, int):
                    raw = qkv[:, p, part, :]
                else:
                    raw = qkv[:, bass.ds(p, 1), part, :].rearrange("p a n -> p (a n)")
                raw = raw.rearrange("p (m h f) -> p m h f", h=2, f=HEAD_DIM)
                m1 = rope_m[:, 0].rearrange("p m (h f) -> p m h f", h=2)
                m2 = rope_m[:, 1].rearrange("p m (h f) -> p m h f", h=2)
                o = to.rearrange("p m (h f) -> p m h f", h=2)
                for h in range(2):
                    nc.vector.tensor_tensor(m1[:, :, h], raw[:, :, h], cos_t[:, :, :], ALU.mult)
                    ins = nc.vector.tensor_tensor(m2[:, :, h], raw[:, :, h], sin_t[:, :, :], ALU.mult)
                ins.then_inc(rope_ok, 1)
                dve.wait_ge(rope_ok, count)
                m1, m2 = (t.rearrange("p m (h f) -> p (m h) f", h=2) for t in (rope_m[:, 0], rope_m[:, 1]))
                o = to.rearrange("p m (h f) -> p (m h) f", h=2)
                nc.vector.tensor_tensor(o[:, :, 0:HALF], m1[:, :, 0:HALF], m2[:, :, HALF:], ALU.subtract)
                nc.vector.tensor_tensor(o[:, :, HALF:], m1[:, :, HALF:], m2[:, :, 0:HALF], ALU.add).then_inc(rope_ok, 1)

            def rope_pair(p, count):
                rope_part(p, 0, rope_q, count + 1)
                dve.wait_ge(rope_ok, count + 2)
                rope_part(p, 1, rope_k, count + 3)

            dve.wait_ge(trig_ok, 4)
            dve.wait_ge(qkv_evac, 2 * TT)
            rope_pair(0, 0)

            def least(p, head):
                for n, i in enumerate(S_ORDER):
                    if n != 1:
                        count = p * 6 + (3 * head + max(n, 1))
                        if not isinstance(p, int):
                            dve.to_reg(count)
                        dve.wait_ge(mask_ok, 1)
                        dve.wait_ge(scores, count)
                    a, w = S_AT[i], P * (i + 1)
                    e = 4 * head + n
                    dve.tensor_tensor_reduce(probs[:, a:a + w], mask[:, S - w:S], ps[:, SB + a:SB + a + w], 1.0,
                                             3.0e38, ALU.add, ALU.min, rmin[:, e:e + 1]).then_inc(row_min, 1)

            def normalise(p, head, count):
                dve.wait_ge(exps, p * 8 + (4 * head + 4))
                nc.vector.reciprocal(prec[:, 4 * head:4 * head + 4], psums[:, 4 * head:4 * head + 4]).then_inc(p_norm, 1)
                dve.wait_ge(p_norm, p * 4 + (2 * head + 1))
                for n, i in enumerate(S_ORDER):
                    a, w = S_AT[i], P * (i + 1)
                    e = 4 * head + n
                    ins = nc.vector.tensor_scalar(probs[:, a:a + w], probs[:, a:a + w], prec[:, e:e + 1], None, ALU.mult)
                ins.then_inc(p_norm, 1)

            def low_probs(p, head):
                dve.wait_ge(p_hi, p * 2 + (head + 1))
                nc.vector.tensor_tensor(pt_lo[:, :], ps[:, TB:TB + TRI], pt_hi[:, :].bitcast(F32), ALU.subtract
                                        ).then_inc(p_lo, 1)

            dve.wait_ge(mask_ok, 1)

            def column(p, row, last):
                return prmT[:, row + p:row + p + 1] if last else prmT[:, bass.ds(p + row, 1)]

            def turn(p, last):
                dve.wait_ge(qk_hi, p * 6 + 2)
                for head in range(2):
                    a, b = head * 64, head * 64 + 64
                    o = (1 - head) * 64
                    nc.vector.scalar_tensor_tensor(out=qs[o:o + 64, head, :], in0=bank(5, p0=a, p1=b),
                                                   scalar=-(HEAD_DIM ** -0.5), in1=qs[a:b, head, :].bitcast(F32),
                                                   op0=ALU.mult, op1=ALU.subtract)
                    if head == 0:
                        dve.wait_ge(qk_hi, p * 6 + 6)
                    for to in range(2):
                        ins = nc.vector.tensor_tensor(k_lo[to * 64:to * 64 + 64, head, :], bank(6, p0=a, p1=b),
                                                      k_hi[a:b, head, :].bitcast(F32), ALU.subtract)
                    ins.then_inc(qk_split, 1)
                least(p, 0)
                normalise(p, 0, 0)
                least(p, 1)
                low_probs(p, 0)
                normalise(p, 1, 0)
                dve.wait_ge(c_copy, p + 1)
                dve.wait_ge(tile_out, p * NT + (H_ + 1))
                nc.vector.tensor_tensor(u[:, CONV_TAPS - 1:], cz[:, :], bank(1), ALU.mult).then_inc(u_ok, 1)
                dve.wait_ge(u_ok, p + 1)
                for tap in range(CONV_TAPS):
                    wc = column(p, 40 + NP * tap, last)
                    if tap == 0:
                        nc.vector.tensor_scalar(yc[:, :], u[:, 0:S], wc, None, ALU.mult).then_inc(tap_ok, 1)
                    else:
                        nc.vector.scalar_tensor_tensor(out=yc[:, :], in0=u[:, tap:tap + S], scalar=wc, in1=yc[:, :],
                                                       op0=ALU.mult, op1=ALU.add).then_inc(tap_ok, 1)
                    dve.wait_ge(tap_ok, p * 3 + (tap + 1))
                dve.wait_ge(tile_out, p * NT + (B_ + 1))
                nc.vector.tensor_tensor(yc[:, :], yc[:, :], bank(0), ALU.mult).then_inc(y_conv, 1)
                dve.wait_ge(y_tmp, p * 2 + 1)
                nc.vector.tensor_tensor(ya[0:64, :], ytmp[0:64, :], bank(2, p0=0, p1=64), ALU.add).then_inc(y_attn, 1)
                low_probs(p, 1)
                dve.wait_ge(bank1_free, p + 2)
                dve.wait_ge(v_lo, p * 2 + 2)
                dve.wait_ge(y_conv, p + 1)
                nc.vector.scalar_tensor_tensor(out=yg[:, :], in0=yc[:, :], scalar=column(p, 36, last), in1=cz[:, :],
                                               op0=ALU.mult, op1=ALU.mult).then_inc(y_gated, 1)
                if not last:
                    rope_pair(p + 1, p * 4 + 4)
                dve.wait_ge(y_tmp, p * 2 + 2)
                nc.vector.tensor_tensor(ya[64:128, :], ytmp[64:128, :], bank(3, p0=64, p1=128), ALU.add
                                        ).then_inc(y_attn, 1)
                dve.wait_ge(bank0_free, p + 2)
                dve.wait_ge(y_lo, p * 2 + 1)
                dve.wait_ge(y_attn, p * 2 + 2)
                nc.vector.scalar_tensor_tensor(out=yg[:, :], in0=ya[:, :], scalar=column(p, 32, last), in1=za[:, :],
                                               op0=ALU.mult, op1=ALU.mult).then_inc(y_gated, 1)

            with dve.Fori(0, NP - 1) as p:
                turn(p, False)
            turn(NP - 1, True)

            dve.wait_ge(ssq_out, 1)
            nc.vector.tensor_scalar(small[:, 40:48], bank(7, 0, 8), 1.0 / DA, EPS, ALU.mult, ALU.add
                                    ).then_inc(ssq_ok, 1)
            dve.wait_ge(gate_ok, 4)
            dve.wait_ge(x2_in, 16 * TT)
            dve.wait_ge(gfin_in, 16)
            for n in range(2):
                for m in range(TT):
                    dve.wait_ge(conv_evac, n * TT + m + 1)
                    dve.wait_ge(attn_out, n * TT + m + 1)
                    o = om[:, m % 2]
                    nc.vector.scalar_tensor_tensor(out=o, in0=bank(4 + m), scalar=rs[:, TT + m:TT + m + 1],
                                                   in1=oc[:, m], op0=ALU.mult, op1=ALU.add).then_inc(attn_evac, 1)
                    dve.wait_ge(attn_evac, n * TT + m + 1)
                    step(nc.vector.tensor_tensor(o, o, gate[:, n * BANK:(n + 1) * BANK], ALU.mult))
                    xs = x2[:, m, n * BANK:(n + 1) * BANK]
                    nc.vector.tensor_tensor(xs, xs, o, ALU.add).then_inc(x2_ok, 1)
                    if n:
                        dve.wait_ge(x2_sq, TT + m + 1)
                        step(nc.vector.tensor_tensor(small[:, 48 + m:49 + m], ss2[:, m:m + 1],
                                                     ss2[:, TT + m:TT + m + 1], ALU.add))
                        nc.vector.tensor_scalar(small[:, 48 + m:49 + m], small[:, 48 + m:49 + m], 1.0 / D, EPS,
                                                ALU.mult, ALU.add).then_inc(fin_ss, 1)
                        dve.wait_ge(fin_rs, m + 1)
                        nc.vector.scalar_tensor_tensor(out=x2[:, m, :], in0=x2[:, m, :], scalar=small[:, 56 + m:57 + m],
                                                       in1=gfin[:, :], op0=ALU.mult, op1=ALU.mult).then_inc(fin_ok, 1)

        @block.tensor
        def _(pe):
            def mm3(o, a_hi, a_lo, b_hi, b_lo, start, stop):
                nc.tensor.matmul(o, a_hi, b_lo, start=start, stop=False)
                nc.tensor.matmul(o, a_lo, b_hi, start=False, stop=False)
                return nc.tensor.matmul(o, a_hi, b_hi, start=False, stop=stop)

            pe.wait_ge(ident_ok, 1)
            pe.wait_ge(prm_in, 16 * 5)
            nc.tensor.transpose(bank(6, 0, 52), prm[0:52, :], ident[0:52, 0:52]).then_inc(prm_tr, 1)
            pe.wait_ge(ones_ok, 1)

            def x_tile(j):
                if j == 0:
                    pe.wait_ge(x_norm, TT)
                else:
                    if j >= 2:
                        pe.wait_ge(h_ok, j - 1)
                for m in range(TT):
                    ins = nc.tensor.transpose(bank(4 + j % 2, m * P, (m + 1) * P), xt[:, m, j * P:(j + 1) * P],
                                              ident[:, :])
                ins.then_inc(x_tr, 1)

            def mod_tile(j):
                pe.wait_ge(chain, RV * (j + 1))
                pe.wait_ge(prods, 2 * (j + 1))
                if j == 0:
                    pe.wait_ge(prm_ok, 1)
                if j >= 2:
                    pe.wait_ge(mod_ok, 2 * (j - 1))
                for two in range(2):
                    o = bank(6 + j % 2, two, two + 1)
                    nc.tensor.matmul(o, acc[:, j % 2, two, :], ones[:, 0:1], start=True, stop=False)
                    nc.tensor.matmul(o, prod[:, j % 2, 0, two, :], ones[:, 0:1], start=False, stop=False)
                    ins = nc.tensor.matmul(o, prod[:, j % 2, 1, two, :], ones[:, 0:1], start=False, stop=True)
                ins.then_inc(mod_sum, 1)

            def slab(g, k):
                for m in range(TT):
                    if not isinstance(g, int) and k == 0:
                        pe.wait_ge(qkv_evac, g * TT + (m + 1 - TT))
                    t = slice(m * P, (m + 1) * P)
                    ins = mm3(bank(m), h_hi[:, k, t], h_lo[:, k, t], w_hi[:, k, :], w_lo[:, k, :], k == 0, k == KT - 1)
                    if k == KT - 1:
                        ins.then_inc(qkv_out, 1)
                if k < KT - 1:
                    ins.then_inc(slab_used, 1)

            x_tile(0)
            mod_tile(0)
            for j in range(KT):
                if j + 1 < KT:
                    x_tile(j + 1)
                    mod_tile(j + 1)
                pe.wait_ge(slab_lo, j + 1)
                pe.wait_ge(hlo_ok, j + 1)
                slab(0, j)
            pe.wait_ge(posf_ok, 1)
            pe.wait_ge(mod_ok, 2 * KT)
            nc.tensor.transpose(bank(6, 0, TT), posf[0:TT, :], ident[0:TT, 0:TT]).then_inc(pos_tr, 1)

            with pe.Fori(1, 3) as g:
                for k in range(KT):
                    pe.wait_ge(slab_lo, g * KT + (k + 1))
                    slab(g, k)
                for i in range(2):
                    pe.wait_ge(chain, g * (2 * R) + (RV * KT - 2 * R + (i + 1) * R))
                    if i == 0:
                        pe.wait_ge(h_ok, KT)
                    nc.tensor.matmul(bank(4 + i, 0, 256), ones[:, :], acc[:, i].rearrange("p a n -> p (a n)"),
                                     start=True, stop=True).then_inc(gate_sum, 1)

            BANK_FREE = [bank0_free, bank1_free, c_copy, u_ok, y_conv]

            def tile(p, t, free):
                pe.wait_ge(tile_lo, p * NT + (t + 1))
                pe.wait_ge(BANK_FREE[t], free)
                for k in range(KT):
                    ins = mm3(bank(TILE_BANK[t]), t_hi[:, t, k], t_lo[:, t, k], h_hi[:, k], h_lo[:, k],
                              k == 0, k == KT - 1)
                ins.then_inc(tile_out, 1)

            def score(p, head):
                for n, i in enumerate(S_ORDER):
                    o = ps[:, SB + S_AT[i]:SB + S_AT[i] + P * (i + 1)]
                    q = qs[:, head, i * P:(i + 1) * P]
                    nc.tensor.matmul(o, q, k_lo[:, head, 0:P * (i + 1)], start=True, stop=False)
                    ins = nc.tensor.matmul(o, q, k_hi[:, head, 0:P * (i + 1)], start=False, stop=True)
                    if n:
                        ins.then_inc(scores, 1)

            def transpose_probs():
                for i in range(TT):
                    for j in range(i + 1):
                        a = S_AT[i] + j * P
                        o = TB + T_AT[j] + (i - j) * P
                        ins = nc.tensor.transpose(ps[:, o:o + P], probs[:, a:a + P], ident[:, :])
                ins.then_inc(p_tr, 1)

            def values(head):
                for j in range(TT):
                    for n, pt in enumerate((pt_lo, pt_hi)):
                        ins = nc.tensor.matmul(bank(2 + head, j * P, BANK), v2[:, head, j, :],
                                               pt[:, T_AT[j]:T_AT[j] + S - j * P],
                                               start=(j == 0 and n == 0), stop=(j == TT - 1 and n == 1))
                ins.then_inc(pv_out, 1)

            def turn(p):
                tile(p, C_, p + 1)
                for n, (src, b) in enumerate(((rope_q, 5), (rope_k, 6))):
                    pe.wait_ge(rope_ok, p * 4 + (2 * n + 2))
                    if n == 0:
                        pe.wait_ge(gate_ok, 4)
                    for m in range(TT):
                        ins = nc.tensor.transpose(bank(b, m * P, (m + 1) * P), src[:, m, :], ident[:, :])
                    ins.then_inc(qk_tr, 1)
                tile(p, H_, p + 1)
                pe.wait_ge(qk_split, p * 2 + 1)
                score(p, 0)
                tile(p, B_, p + 1)
                pe.wait_ge(p_norm, p * 4 + 2)
                transpose_probs()
                pe.wait_ge(qk_split, p * 2 + 2)
                score(p, 1)
                tile(p, ZC, p + 1)
                pe.wait_ge(p_lo, p * 2 + 1)
                pe.wait_ge(v_lo, p * 2 + 2)
                pe.wait_ge(row_min, p * 8 + 8)
                values(0)
                pe.wait_ge(p_norm, p * 4 + 4)
                transpose_probs()
                tile(p, ZA, p + 1)
                pe.wait_ge(p_lo, p * 2 + 2)
                values(1)

            with pe.Fori(0, NP - 1) as p:
                turn(p)
            turn(NP - 1)

            def project(n, part, m, b, rows):
                t = slice(m * P, (m + 1) * P)
                for k in range(NP):
                    ins = mm3(bank(b), y[:, k, part, t], y[:, k, part + 1, t], w_hi[:, rows + k], w_lo[:, rows + k],
                              k == 0, k == NP - 1)
                return ins

            pe.wait_ge(slab_lo, 4 * KT)
            pe.wait_ge(y_lo, 2 * NP - 1)
            pe.wait_ge(y_attn, 2 * NP)
            pe.wait_ge(bank0_free, NP + 1)
            pe.wait_ge(bank1_free, NP + 1)
            for m in range(TT):
                project(0, 2, m, m, NP).then_inc(conv_out, 1)
            pe.wait_ge(sq_added, 2 * NP + 1)
            for part in range(2):
                for m in range(TT):
                    ins = nc.tensor.matmul(bank(7, part * TT + m, part * TT + m + 1), sqsum[:, part, m * P:(m + 1) * P],
                                           ones[:, 0:1], start=True, stop=True)
            ins.then_inc(ssq_out, 1)
            pe.wait_ge(y_lo, 2 * NP)
            for m in range(TT):
                if m == 3:
                    pe.wait_ge(ssq_ok, 1)
                project(0, 0, m, 4 + m, 0).then_inc(attn_out, 1)
            pe.wait_ge(slab_lo, 4 * KT + 4)
            for m in range(TT):
                pe.wait_ge(conv_evac, m + 1)
                project(1, 2, m, m, NP).then_inc(conv_out, 1)
            pe.wait_ge(slab_lo, 5 * KT)
            for m in range(TT):
                pe.wait_ge(attn_evac, m + 1)
                project(1, 0, m, 4 + m, 0).then_inc(attn_out, 1)


_INS = ["x", "c", "positions", "w_ada", "b_ada", "g_norm", "w_in", "w_conv", "g_attn_out", "g_conv_out",
        "w_out", "g_final"]


def kernel(**inputs):
    import numpy as np
    import concourse.bacc as bacc
    from concourse.bass_utils import run_bass_kernel_spmd as run

    nc = bacc.Bacc("TRN2", target_bir_lowering=False, num_devices=1, dynamic_dma_scratch_size=64)
    arrays, args = {}, []
    given = [(name, np.ascontiguousarray(inputs[name])) for name in _INS]
    half = HEAD_DIM // 2
    given.append(("inv_freq", (10000.0 ** (-np.arange(half) / half)).astype(np.float32)))
    for name, a in given:
        arrays[f"in_{name}"] = a
        args.append(nc.dram_tensor(f"in_{name}", a.shape, mybir.dt.from_np(a.dtype), kind="ExternalInput").ap())
    shape = inputs["x"].shape
    args.append(nc.dram_tensor("out_0", shape, F32, kind="ExternalOutput").ap())
    build(nc, *args)
    r = run(nc, [arrays], core_ids=[0])
    return r.results[0]["out_0"]
```

```python
from contextlib import ExitStack

import concourse.bass as bass
from concourse import mybir

F32 = mybir.dt.float32
F32R = mybir.dt.float32r
I32 = mybir.dt.int32
ALU = mybir.AluOpType
ACT = mybir.ActivationFunctionType

P = 128
BANK = 512
HEAD_DIM = 64
CONV_TAPS = 3
EPS = 1e-6
MASKED = 1e30
PI = 3.141592653589793
TWO_PI_INV = 1.0 / (2.0 * PI)
ROUND = 1.5 * 2.0 ** 23
PI_BELOW = 3.1415925


def two_pi_pieces(bits, low):
    pieces, rest, unit = [], 2.0 * PI, 2.0 ** (3 - bits)
    while unit >= low:
        piece = int(rest / unit) * unit
        if piece:
            pieces.append(piece)
        rest -= piece
        unit /= 2.0 ** bits
    return pieces


def build(nc, x, c, positions, w_ada, b_ada, g_norm, w_in, w_conv, g_attn_out, g_conv_out,
          w_out, g_final, inv_freq, out):
    _, S, D = x.shape
    DA = g_attn_out.shape[0]
    KT = D // P
    TT = S // P
    NP = DA // P
    HALF = HEAD_DIM // 2
    R = D // P
    GC = D // 256
    assert S == BANK and KT == 8 and TT == 4 and NP == 4 and D == 2 * BANK

    B_, ZC, ZA, CN, HN = range(5)
    COLS = [4 * DA, 7 * DA, 3 * DA, 5 * DA, 6 * DA]
    NT = len(COLS)
    TILE_BANK = [0, 1, 0, 4, 5]
    RAW_SLOT = [0, 1, 2, 0, 1]
    C_BANK, H_BANK = TILE_BANK[CN], TILE_BANK[HN]
    Q_BANK, K_BANK = 6, 7
    CONV_BANK, ATTN_BANK = [1, 4, 0, 2], [5, 6, 3, 7]

    S_AT = {3: 0, 2: 512, 0: 896, 1: 1024}
    T_AT = {0: 0, 1: 512, 3: 896, 2: 1024}
    S_ORDER = [2, 0, 3, 1]
    TRI = 1280
    SB, TB = 2 * BANK, 5 * BANK

    with ExitStack() as ctx:
        cursor = [(nc.sbuf_base + 31) // 32 * 32]

        def at(name, offset, shape, dt=F32):
            return nc.alloc_sbuf_tensor_at(name, [P, *shape], dt, offset=offset)

        def sb(name, shape, dt=F32):
            size = 4
            for n in shape:
                size *= n
            offset = cursor[0]
            cursor[0] = (offset + size + 31) // 32 * 32
            return at(name, offset, shape, dt)

        def sem(name):
            return ctx.enter_context(nc.semaphore(name))

        h_hi = sb("h_hi", [KT, S], F32R)
        h_lo = sb("h_lo", [KT, S], F32R)
        w_hi = sb("w_hi", [8, BANK], F32R)
        w_lo = sb("w_lo", [8, BANK], F32R)
        w_raw = sb("w_raw", [4, BANK])
        tile_raw = sb("tile_raw", [3, KT, P])
        rope_q = sb("rope_q", [TT, P])
        rope_k = sb("rope_k", [TT, P])
        cos_t = sb("cos_t", [TT, HEAD_DIM])
        sin_t = sb("sin_t", [TT, HEAD_DIM])
        rope_m = sb("rope_m", [2, TT, P])
        ch_hi = at("ch_hi", cursor[0], [2, 2, P], F32R)
        qs = sb("qs", [2, S], F32R)
        ch_lo = at("ch_lo", cursor[0], [2, 2, P], F32R)
        k_hi = sb("k_hi", [2, S], F32R)
        ch_raw = at("ch_raw", cursor[0], [4, 2, P])
        k_lo = sb("k_lo", [2, S], F32R)
        pt_hi = sb("pt_hi", [TRI], F32R)
        gate_acc = at("gate_acc", cursor[0], [GC, 256])
        pt_lo = sb("pt_lo", [TRI], F32R)
        v2 = sb("v2", [2, TT, P], F32R)
        cz = sb("cz", [S])
        u = sb("u", [S + CONV_TAPS - 1])
        yc = sb("yc", [S])
        invf = at("invf", cursor[0], [HALF])
        ang = at("ang", cursor[0] + 4 * HALF, [TT, HALF])
        turns = at("turns", cursor[0] + 4 * HALF * (TT + 1), [TT, HALF])
        yg = sb("yg", [S])
        ya = sb("ya", [S])
        za = sb("za", [S])
        ytmp = at("ytmp", cursor[0], [S])
        sq = sb("sq", [S])
        sqsum = sb("sqsum", [2, S])
        mask = sb("mask", [S])
        probs = sb("probs", [TRI])
        ident = sb("ident", [P])
        ones = sb("ones", [P])
        gate = sb("gate", [D])
        prmT = sb("prmT", [64])
        cs = sb("cs", [R])
        sc = sb("sc", [R])
        gs = sb("gs", [KT])
        sh = sb("sh", [KT])
        b1 = sb("b1", [KT])
        small = sb("small", [64])
        rmin = sb("rmin", [8])
        psums = sb("psums", [8])
        prec = sb("prec", [8])
        rs = sb("rs", [8])
        ss2 = sb("ss2", [8])
        posT = sb("posT", [TT])
        base = cursor[0]
        sb("y_", [NP, 4, S])
        xt = at("xt", base, [TT, D])
        qkv = at("qkv", base, [NP, 4, S])
        y = at("y", base, [NP, 4, S], F32R)
        base = cursor[0]
        sb("tile_", [2 * NT, KT * P])
        t_hi = at("t_hi", base, [NT, KT, P], F32R)
        t_lo = at("t_lo", base + NT * KT * P * 4, [NT, KT, P], F32R)
        ada = at("ada", base, [3, 2, R, P])
        acc = at("acc", base + 24576, [2, 2, P])
        h32 = at("h32", base + 30720, [2, S])
        junk = at("junk", base + 34816, [D])
        x2 = at("x2", base, [TT, D])
        gfin = at("gfin", base + 16384, [D])
        oc = at("oc", base + 20480, [TT, BANK])
        om = at("om", base + 28672, [2, BANK])
        junk2 = at("junk2", base + 32768, [BANK])
        prm = at("prm", base + 38912, [P])
        posi = at("posi", base + 39424, [P], I32)
        posf = at("posf", base + 39936, [P])
        assert cursor[0] <= nc.sbuf_usable_end, (cursor[0], nc.sbuf_usable_end)

        ps = ctx.enter_context(nc.psum_tensor("ps", [P, 8 * BANK], F32))

        def bank(b, lo=0, hi=BANK, p0=0, p1=P):
            return ps[p0:p1, b * BANK + lo:b * BANK + hi]

        c_in, pos_in, prm_in, gate_in = sem("c_in"), sem("pos_in"), sem("prm_in"), sem("gate_in")
        x_in = [sem(f"x_in{m}") for m in range(TT)]
        ada_in = [sem(f"ada_in{i}") for i in range(3)]
        raw_in = [sem(f"raw_in{i}") for i in range(4)]
        ch_in = [sem(f"ch_in{i}") for i in range(4)]
        tile_in = [sem(f"tile_in{i}") for i in range(3)]
        x2_in, gfin_in, out_done = sem("x2_in"), sem("gfin_in"), sem("out_done")
        ident_ok, mask_ok, ones_ok, pool_step = sem("ident_ok"), sem("mask_ok"), sem("ones_ok"), sem("pool_step")
        silu_c, x_sq, x_rstd, x_norm = sem("silu_c"), sem("x_sq"), sem("x_rstd"), sem("x_norm")
        prm_tr, pos_tr, prm_ok, posf_ok = sem("prm_tr"), sem("pos_tr"), sem("prm_ok"), sem("posf_ok")
        chain, mod_sum, mod_ok = sem("chain"), sem("mod_sum"), sem("mod_ok")
        x_tr, h_ok, hhi_ok, hlo_ok = sem("x_tr"), sem("h_ok"), sem("hhi_ok"), sem("hlo_ok")
        slab_hi, slab_lo, slab_used, ch_used = sem("slab_hi"), sem("slab_lo"), sem("slab_used"), sem("ch_used")
        qkv_out, qkv_evac, gate_sum, gate_ok = sem("qkv_out"), sem("qkv_evac"), sem("gate_sum"), sem("gate_ok")
        dve_step, angle_ok, trig_ok, rope_ok = sem("dve_step"), sem("angle_ok"), sem("trig_ok"), sem("rope_ok")
        tile_hi, tile_lo, tile_out = sem("tile_hi"), sem("tile_lo"), sem("tile_out")
        bank0_free, bank1_free, u_ok, tap_ok = sem("bank0_free"), sem("bank1_free"), sem("u_ok"), sem("tap_ok")
        qk_tr, qk_hi, qk_split, v_hi, v_lo = sem("qk_tr"), sem("qk_hi"), sem("qk_split"), sem("v_hi"), sem("v_lo")
        scores, row_min, exps, p_norm = sem("scores"), sem("row_min"), sem("exps"), sem("p_norm")
        p_tr, p_hi, p_lo, pv_out = sem("p_tr"), sem("p_hi"), sem("p_lo"), sem("pv_out")
        y_tmp, y_attn, c_copy, y_conv = sem("y_tmp"), sem("y_attn"), sem("c_copy"), sem("y_conv")
        y_gated, y_hi, y_lo = sem("y_gated"), sem("y_hi"), sem("y_lo")
        sq_ok, sq_added = sem("sq_ok"), sem("sq_added")
        ssq_out, ssq_ok, rs_ok = sem("ssq_out"), sem("ssq_ok"), sem("rs_ok")
        conv_out, attn_out, conv_evac, attn_evac = sem("conv_out"), sem("attn_out"), sem("conv_evac"), sem("attn_evac")
        conv_added = sem("conv_added")
        x2_ok, x2_sq, x2_g, ss2_eps, fin_rs = sem("x2_ok"), sem("x2_sq"), sem("x2_g"), sem("ss2_eps"), sem("fin_rs")
        fin_left, fin_right = sem("fin_left"), sem("fin_right")

        w_ada_v = w_ada.rearrange("(p r) n -> p r n", r=R)
        w_in_v = w_in.rearrange("(k p) n -> k p n", p=P)
        w_in_t = w_in.rearrange("(k p) n -> p k n", p=P)
        w_out_v = w_out.rearrange("(k p) n -> k p n", p=P)

        block = ctx.enter_context(nc.Block())

        @block.sync
        def _(sp):
            sp.dma_start(posi[0:TT, :], positions.rearrange("a (t p) -> (a t) p", p=P)).then_inc(pos_in, 16)
            sp.dma_start(invf[:, :], inv_freq.partition_broadcast(P)).then_inc(pos_in, 16)
            for m in range(TT):
                sp.dma_start(xt[:, m, :], x[0, m * P:(m + 1) * P, :]).then_inc(x_in[m], 16)
                if m == 0:
                    sp.dma_start(cs[:, :], c.rearrange("a (p r) -> p (a r)", r=R)).then_inc(c_in, 16)
            row = 0
            for src in (b_ada.rearrange("(t p) -> t p", p=P), g_norm.rearrange("(t p) -> t p", p=P),
                        g_attn_out.rearrange("(t p) -> t p", p=P), g_conv_out.rearrange("(t p) -> t p", p=P),
                        w_conv.rearrange("a (t p) -> (a t) p", p=P)):
                n = src.shape[0]
                sp.dma_start(prm[row:row + n, :], src).then_inc(prm_in, 16)
                row += n
            for j in range(KT + GC):
                if j >= 3:
                    sp.wait_ge(chain, R * (j - 2))
                for two in range(2):
                    col = (1 - two) * D + j * P if j < KT else 2 * D + (2 * (j - KT) + two) * P
                    sp.dma_start(ada[:, j % 3, two], w_ada_v[:, :, col:col + P]).then_inc(ada_in[j % 3], 16)
                for k in ([j] if j < KT else [2 * j - KT, 2 * j - KT + 1]):
                    if k >= 4:
                        sp.wait_ge(slab_lo, k - 3)
                    g = k // KT
                    sp.dma_start(w_raw[:, k % 4], w_in_v[k % KT, :, g * BANK:(g + 1) * BANK]
                                 ).then_inc(raw_in[k % 4], 16)
                if j < KT:
                    sp.dma_start(ch_raw[:, j % 4],
                                 w_in_v[j, :, COLS[CN]:COLS[CN] + 2 * DA].rearrange("p (two n) -> p two n", two=2)[:, :, 0:P]
                                 ).then_inc(ch_in[j % 4], 16)
            sp.dma_start(gate[:, :], b_ada[2 * D:3 * D].partition_broadcast(P)).then_inc(gate_in, 16)
            for t in (B_, ZC, ZA):
                sp.dma_start(tile_raw[:, RAW_SLOT[t]], w_in_t[:, :, COLS[t]:COLS[t] + P]
                             ).then_inc(tile_in[RAW_SLOT[t]], 16)
            for k in range(KT):
                sp.wait_ge(slab_lo, 2 * KT + k - 3)
                sp.dma_start(w_raw[:, k % 4], w_in_v[k, :, 2 * BANK:3 * BANK]).then_inc(raw_in[k % 4], 16)

            def turn(p, last):
                for n, (t, split) in enumerate([] if last else [(CN, 1), (HN, 2), (ZA, 3), (B_, 4), (ZC, 5)]):
                    sp.wait_ge(tile_lo, p * NT + split)
                    sp.dma_start(tile_raw[:, RAW_SLOT[t]],
                                 w_in_t[:, :, bass.ds(p * P + (COLS[t] + P), P)]
                                 ).then_inc(tile_in[RAW_SLOT[t]], 16)
                for i in range(2):
                    sp.wait_ge(slab_lo, p * 2 + 3 * KT)
                    sp.dma_start(w_raw[:, i], w_out_v[bass.ds(p * 2 + i, 1), :, 0:BANK].rearrange("a p n -> p (a n)")
                                 ).then_inc(raw_in[i], 16)

            with sp.Fori(0, NP - 1) as p:
                turn(p, False)
            turn(NP - 1, True)
            sp.wait_ge(slab_lo, 4 * KT)
            for k in (4, 5, 6, 7):
                sp.dma_start(w_raw[:, k % 4], w_out_v[k, :, BANK:D]).then_inc(raw_in[k % 4], 16)
            sp.wait_ge(tile_out, NT * NP)
            for m in range(TT):
                sp.dma_start(x2[:, m, :], x[0, m * P:(m + 1) * P, :]).then_inc(x2_in, 16)
            sp.dma_start(gfin[:, :], g_final.partition_broadcast(P)).then_inc(gfin_in, 16)
            for k in (0, 1, 2, 3):
                sp.wait_ge(slab_lo, 4 * KT + k + 1)
                sp.dma_start(w_raw[:, k % 4], w_out_v[k, :, BANK:D]).then_inc(raw_in[k % 4], 16)
            for m in range(TT):
                sp.wait_ge(fin_left, m + 1)
                sp.wait_ge(fin_right, m + 1)
                sp.dma_start(out[0, m * P:(m + 1) * P, :], x2[:, m, :]).then_inc(out_done, 16)
            sp.wait_ge(out_done, 16 * TT)

        @block.scalar
        def _(act):
            for m in range(TT):
                act.wait_ge(x_in[m], 16)
                if m:
                    act.wait_ge(x_sq, m)
                nc.scalar.activation(junk[:, :], xt[:, m, :], ACT.Square, scale=D ** -0.5,
                                     accum_out=small[:, m:m + 1]).then_inc(x_sq, 1)
                if m == 0:
                    act.wait_ge(c_in, 16)
                    nc.scalar.activation(sc[:, :], cs[:, :], ACT.Silu).then_inc(silu_c, 1)

            for j in range(KT):
                act.wait_ge(raw_in[j % 4], 16 * (j // 4 + 1))
                nc.scalar.activation(w_hi[:, j], w_raw[:, j % 4], ACT.Copy)
                act.wait_ge(ch_in[j % 4], 16 * (j // 4 + 1))
                if j >= 2:
                    act.wait_ge(ch_used, j - 1)
                nc.scalar.activation(ch_hi[:, j % 2], ch_raw[:, j % 4], ACT.Copy).then_inc(slab_hi, 1)
                act.wait_ge(h_ok, j + 1)
                nc.scalar.activation(h_hi[:, j], h32[:, j % 2], ACT.Copy).then_inc(hhi_ok, 1)
                if j == 1:
                    act.wait_ge(angle_ok, 1)
                    sin_v = sin_t.rearrange("p m (two f) -> p m two f", two=2)
                    cos_v = cos_t.rearrange("p m (two f) -> p m two f", two=2)
                    for two in range(2):
                        nc.scalar.activation(sin_v[:, :, two, :], ang[:, :, :], ACT.Sin).then_inc(trig_ok, 1)
                        nc.scalar.activation(cos_v[:, :, two, :], turns[:, :, :], ACT.Sin).then_inc(trig_ok, 1)
            act.wait_ge(tile_out, 1)
            nc.scalar.activation(cz[:, :], bank(C_BANK), ACT.Copy).then_inc(c_copy, 1)

            def evacuate(g, m):
                act.wait_ge(x_sq, TT)
                act.wait_ge(qkv_out, g * TT + (m + 1))
                out_ap = qkv[:, :, g, m * P:(m + 1) * P] if isinstance(g, int) else \
                    qkv[:, :, bass.ds(g, 1), m * P:(m + 1) * P].rearrange("p a g n -> p a (g n)")
                ins = nc.scalar.activation(out_ap, bank(m).rearrange("p (a n) -> p a n", n=P), ACT.Copy)
                ins.then_inc(qkv_evac, 1)

            with act.Fori(1, 3) as g:
                for k in range(KT):
                    if k < KT - 1:
                        act.wait_ge(slab_used, g * (KT - 1) + (k + 1 - (KT - 1)))
                    else:
                        for m in range(TT):
                            evacuate(g - 1, m)
                    act.wait_ge(raw_in[k % 4], g * 32 + 16 * (k // 4 + 1))
                    nc.scalar.activation(w_hi[:, k], w_raw[:, k % 4], ACT.Copy).then_inc(slab_hi, 1)
            act.wait_ge(chain, R * (KT + GC))

            def split_tile(t, arrived):
                act.wait_ge(tile_in[RAW_SLOT[t]], arrived)
                nc.scalar.activation(t_hi[:, t], tile_raw[:, RAW_SLOT[t]], ACT.Copy).then_inc(tile_hi, 1)

            for t in (B_, ZC, ZA):
                split_tile(t, 16)
            for m in range(TT):
                act.wait_ge(qkv_out, 2 * TT + m + 1)
                ins = nc.scalar.activation(qkv[:, :, 2, m * P:(m + 1) * P],
                                           bank(m).rearrange("p (a n) -> p a n", n=P), ACT.Copy)
                ins.then_inc((bank0_free, bank1_free, qkv_evac, qkv_evac)[m], 1)
            act.wait_ge(bank0_free, 1)
            act.wait_ge(bank1_free, 1)
            act.wait_ge(qkv_evac, 2 * TT + 2)

            def exponents(p, head):
                for n, i in enumerate(S_ORDER):
                    act.wait_ge(row_min, p * 8 + (4 * head + n + 1))
                    a, w = S_AT[i], P * (i + 1)
                    e = 4 * head + n
                    nc.scalar.activation(probs[:, a:a + w], probs[:, a:a + w], ACT.Exp, scale=-1.0,
                                         bias=rmin[:, e:e + 1], accum_out=psums[:, e:e + 1]).then_inc(exps, 1)

            def turn(p, last):
                act.wait_ge(qk_tr, p * 2 + 1)
                for head in range(2):
                    a, b = head * 64, head * 64 + 64
                    nc.scalar.activation(qs[a:b, head, :], bank(Q_BANK, p0=a, p1=b), ACT.Copy,
                                         scale=-(HEAD_DIM ** -0.5)).then_inc(qk_hi, 1)
                act.wait_ge(qk_tr, p * 2 + 2)
                for head in range(2):
                    a, b = head * 64, head * 64 + 64
                    for to in range(2):
                        nc.scalar.activation(k_hi[to * 64:to * 64 + 64, head, :], bank(K_BANK, p0=a, p1=b),
                                             ACT.Copy).then_inc(qk_hi, 1)
                for head in range(2):
                    hc = head * HEAD_DIM
                    src = qkv[:, p, 2, :] if last else qkv[:, bass.ds(p, 1), 2, :].rearrange("p a n -> p (a n)")
                    nc.scalar.activation(v2[:, head, :, hc:hc + HEAD_DIM],
                                         src.rearrange("p (m n) -> p m n", n=P)[:, :, hc:hc + HEAD_DIM],
                                         ACT.Copy).then_inc(v_hi, 1)
                if not last:
                    split_tile(CN, p * 32 + 32)
                exponents(p, 0)
                if not last:
                    split_tile(HN, p * 32 + 32)
                act.wait_ge(p_tr, p * 2 + 1)
                nc.scalar.activation(pt_hi[:, :], ps[:, TB:TB + TRI], ACT.Copy).then_inc(p_hi, 1)
                act.wait_ge(y_conv, p + 1)
                act.wait_ge(sq_added, p * 2 + 1)
                nc.scalar.activation(sq[:, :], yc[:, :], ACT.Square).then_inc(sq_ok, 1)
                exponents(p, 1)
                act.wait_ge(tile_out, p * NT + (ZC + 3))
                nc.scalar.activation(cz[:, :], bank(TILE_BANK[ZC]), ACT.Silu).then_inc(bank1_free, 1)
                if not last:
                    split_tile(B_, p * 32 + 48)
                act.wait_ge(qkv_evac, 2 * TT + 2)
                act.wait_ge(y_gated, p * 2 + 1)
                yp = y[:, p] if last else y[:, bass.ds(p, 1)].rearrange("p a s n -> p (a s) n")
                nc.scalar.activation(yp[:, 2], yg[:, :], ACT.Copy).then_inc(y_hi, 1)
                act.wait_ge(tile_out, p * NT + (ZA + 3))
                nc.scalar.activation(za[:, :], bank(TILE_BANK[ZA]), ACT.Silu).then_inc(bank0_free, 1)
                act.wait_ge(sq_added, p * 2 + 2)
                act.wait_ge(pv_out, p * 2 + 1)
                nc.scalar.activation(ytmp[0:64, :], bank(2, p0=64, p1=128), ACT.Copy).then_inc(y_tmp, 1)
                act.wait_ge(p_tr, p * 2 + 2)
                nc.scalar.activation(pt_hi[:, :], ps[:, TB:TB + TRI], ACT.Copy).then_inc(p_hi, 1)
                if not last:
                    split_tile(ZC, p * 32 + 48)
                for i in range(2):
                    act.wait_ge(qkv_out, 3 * TT)
                    act.wait_ge(raw_in[i], p * 16 + (16 * 6 + 16))
                    nc.scalar.activation(w_hi[:, bass.ds(p * 2 + i, 1)].rearrange("p a n -> p (a n)"),
                                         w_raw[:, i], ACT.Copy).then_inc(slab_hi, 1)
                if not last:
                    split_tile(ZA, p * 16 + 32)
                    act.wait_ge(tile_out, p * NT + (CN + 3))
                    nc.scalar.activation(cz[:, :], bank(C_BANK), ACT.Copy).then_inc(c_copy, 1)
                act.wait_ge(pv_out, p * 2 + 2)
                nc.scalar.activation(ytmp[64:128, :], bank(3, p0=0, p1=64), ACT.Copy).then_inc(y_tmp, 1)
                act.wait_ge(y_gated, p * 2 + 2)
                nc.scalar.activation(yp[:, 0], yg[:, :], ACT.Copy).then_inc(y_hi, 1)
                act.wait_ge(sq_added, p * 2 + 2)
                nc.scalar.activation(sq[:, :], ya[:, :], ACT.Square).then_inc(sq_ok, 1)

            with act.Fori(0, NP - 1) as p:
                turn(p, False)
            turn(NP - 1, True)

            act.wait_ge(conv_out, TT)
            for k in (4, 5, 6, 7):
                act.wait_ge(raw_in[k % 4], 16 * (7 + (4 if k % 4 < 2 else 0)))
                nc.scalar.activation(w_hi[:, k], w_raw[:, k % 4], ACT.Copy).then_inc(slab_hi, 1)
            act.wait_ge(rs_ok, 1)

            def square(n, m):
                act.wait_ge(x2_ok, n * TT + m + 1)
                if n or m:
                    act.wait_ge(x2_sq, n * TT + m)
                nc.scalar.activation(junk2[:, :], x2[:, m, n * BANK:(n + 1) * BANK], ACT.Square, scale=D ** -0.5,
                                     accum_out=ss2[:, n * TT + m:n * TT + m + 1]).then_inc(x2_sq, 1)

            def scale_left(m):
                act.wait_ge(fin_rs, m + 1)
                nc.scalar.activation(x2[:, m, 0:BANK], x2[:, m, 0:BANK], ACT.Copy,
                                     scale=small[:, 56 + m:57 + m]).then_inc(fin_left, 1)

            for n in range(2):
                for m in range(TT):
                    if n:
                        act.wait_ge(attn_evac, m + 1)
                    act.wait_ge(conv_out, n * TT + m + 1)
                    nc.scalar.activation(oc[:, m], bank(CONV_BANK[m]), ACT.Copy, scale=rs[:, m:m + 1]
                                         ).then_inc(conv_evac, 1)
                if n == 0:
                    for m in range(TT):
                        square(0, m)
                    act.wait_ge(attn_out, TT)
                    for k in (0, 1, 2, 3):
                        act.wait_ge(raw_in[k % 4], 16 * (8 + (4 if k % 4 < 2 else 0)))
                        nc.scalar.activation(w_hi[:, k], w_raw[:, k % 4], ACT.Copy).then_inc(slab_hi, 1)
            for m in range(TT):
                square(1, m)
                if m:
                    scale_left(m - 1)
            scale_left(TT - 1)

        @block.gpsimd
        def _(pool):
            nc.gpsimd.memset(ident[:, :], 0.0).then_inc(pool_step, 1)
            nc.gpsimd.memset(mask[:, :], 0.0).then_inc(pool_step, 1)
            nc.gpsimd.memset(small[:, 32:40], -0.5).then_inc(pool_step, 1)
            nc.gpsimd.memset(sqsum[:, :, :], 0.0).then_inc(sq_added, 1)
            pool.wait_ge(pool_step, 1)
            nc.gpsimd.affine_select(out=ident[:, :], in_=ident[:, :], compare_op=ALU.not_equal, fill=1.0, base=0,
                                    pattern=[[-1, P]], channel_multiplier=1).then_inc(ident_ok, 1)
            pool.wait_ge(pool_step, 2)
            nc.gpsimd.affine_select(out=mask[:, S - P:S], in_=mask[:, S - P:S], compare_op=ALU.is_ge, fill=MASKED,
                                    base=0, pattern=[[-1, P]], channel_multiplier=1).then_inc(mask_ok, 1)
            for m in range(TT):
                pool.wait_ge(x_sq, m + 1)
                nc.gpsimd.tensor_scalar(small[:, 8 + m:9 + m], small[:, m:m + 1], EPS, None, ALU.add
                                        ).then_inc(pool_step, 1)
                pool.wait_ge(pool_step, 4 + m)
                nc.gpsimd.tensor_tensor(small[:, 16 + m:17 + m], small[:, 8 + m:9 + m], small[:, 32:33], ALU.pow
                                        ).then_inc(x_rstd, 1)

            for j in range(KT):
                pool.wait_ge(slab_hi, j + 1)
                nc.gpsimd.tensor_tensor(ch_lo[:, j % 2], ch_raw[:, j % 4], ch_hi[:, j % 2].bitcast(F32), ALU.subtract)
                nc.gpsimd.tensor_tensor(w_lo[:, j], w_raw[:, j % 4], w_hi[:, j].bitcast(F32), ALU.subtract
                                        ).then_inc(slab_lo, 1)
                pool.wait_ge(hhi_ok, j + 1)
                nc.gpsimd.tensor_tensor(h_lo[:, j], h32[:, j % 2], h_hi[:, j].bitcast(F32), ALU.subtract
                                        ).then_inc(hlo_ok, 1)
            with pool.Fori(1, 3) as g:
                for k in range(KT):
                    pool.wait_ge(slab_hi, g * KT + (k + 1))
                    nc.gpsimd.tensor_tensor(w_lo[:, k], w_raw[:, k % 4], w_hi[:, k].bitcast(F32), ALU.subtract
                                            ).then_inc(slab_lo, 1)

            def split_tile(t, count):
                pool.wait_ge(tile_hi, count)
                nc.gpsimd.tensor_tensor(t_lo[:, t], tile_raw[:, RAW_SLOT[t]], t_hi[:, t].bitcast(F32), ALU.subtract
                                        ).then_inc(tile_lo, 1)

            for t in (B_, ZC, ZA):
                split_tile(t, t + 1)

            def turn(p, last):
                for head in range(2):
                    pool.wait_ge(v_hi, p * 2 + (head + 1))
                    hc, lc = head * HEAD_DIM, (1 - head) * HEAD_DIM
                    src = qkv[:, p, 2, :] if last else qkv[:, bass.ds(p, 1), 2, :].rearrange("p a n -> p (a n)")
                    nc.gpsimd.tensor_tensor(v2[:, head, :, lc:lc + HEAD_DIM],
                                            src.rearrange("p (m n) -> p m n", n=P)[:, :, hc:hc + HEAD_DIM],
                                            v2[:, head, :, hc:hc + HEAD_DIM].bitcast(F32), ALU.subtract
                                            ).then_inc(v_lo, 1)
                if not last:
                    split_tile(CN, p * NT + 4)
                    split_tile(HN, p * NT + 5)
                pool.wait_ge(sq_ok, p * 2 + 1)
                pool.wait_ge(sq_added, p * 2 + 1)
                nc.gpsimd.tensor_tensor(sqsum[:, 0], sqsum[:, 0], sq[:, :], ALU.add).then_inc(sq_added, 1)
                if not last:
                    split_tile(B_, p * NT + 6)
                yp = y[:, p] if last else y[:, bass.ds(p, 1)].rearrange("p a s n -> p (a s) n")
                pool.wait_ge(y_hi, p * 2 + 1)
                nc.gpsimd.tensor_tensor(yp[:, 3], yg[:, :], yp[:, 2].bitcast(F32), ALU.subtract).then_inc(y_lo, 1)
                if not last:
                    split_tile(ZC, p * NT + 7)
                for i in range(2):
                    pool.wait_ge(slab_hi, p * 2 + (3 * KT + i + 1))
                    s = bass.ds(p * 2 + i, 1)
                    nc.gpsimd.tensor_tensor(w_lo[:, s].rearrange("p a n -> p (a n)"), w_raw[:, i],
                                            w_hi[:, s].rearrange("p a n -> p (a n)").bitcast(F32), ALU.subtract
                                            ).then_inc(slab_lo, 1)
                if not last:
                    split_tile(ZA, p * NT + 8)
                pool.wait_ge(y_hi, p * 2 + 2)
                nc.gpsimd.tensor_tensor(yp[:, 1], yg[:, :], yp[:, 0].bitcast(F32), ALU.subtract).then_inc(y_lo, 1)
                pool.wait_ge(sq_ok, p * 2 + 2)
                nc.gpsimd.tensor_tensor(sqsum[:, 1], sqsum[:, 1], sq[:, :], ALU.add).then_inc(sq_added, 1)

            with pool.Fori(0, NP - 1) as p:
                turn(p, False)
            turn(NP - 1, True)
            pool.wait_ge(slab_hi, 4 * KT + 4)
            for k in (4, 5, 6, 7):
                nc.gpsimd.tensor_tensor(w_lo[:, k], w_raw[:, k % 4], w_hi[:, k].bitcast(F32), ALU.subtract
                                        ).then_inc(slab_lo, 1)
            pool.wait_ge(ssq_ok, 1)
            nc.gpsimd.tensor_tensor(rs[:, :], small[:, 40:48], small[:, 32:40], ALU.pow).then_inc(rs_ok, 1)
            for k in (0, 1, 2, 3):
                pool.wait_ge(slab_hi, 4 * KT + 4 + k + 1)
                nc.gpsimd.tensor_tensor(w_lo[:, k], w_raw[:, k % 4], w_hi[:, k].bitcast(F32), ALU.subtract
                                        ).then_inc(slab_lo, 1)
            pool.wait_ge(x2_sq, TT)
            nc.gpsimd.tensor_scalar(ss2[:, 0:TT], ss2[:, 0:TT], EPS, None, ALU.add).then_inc(ss2_eps, 1)
            pool.wait_ge(gfin_in, 16)
            for m in range(TT):
                nc.gpsimd.tensor_tensor(x2[:, m, 0:BANK], x2[:, m, 0:BANK], gfin[:, 0:BANK], ALU.mult).then_inc(x2_g, 1)
            pool.wait_ge(ss2_eps, 1)
            for m in range(TT):
                pool.wait_ge(x2_sq, TT + m + 1)
                pool.wait_ge(x2_g, m + 1)
                nc.gpsimd.tensor_scalar(small[:, 48 + m:49 + m], ss2[:, TT + m:TT + m + 1], ss2[:, m:m + 1], None,
                                        ALU.add).then_inc(pool_step, 1)
                pool.wait_ge(pool_step, 4 + TT + m)
                nc.gpsimd.tensor_tensor(small[:, 56 + m:57 + m], small[:, 48 + m:49 + m], small[:, 32:33], ALU.pow
                                        ).then_inc(fin_rs, 1)

        @block.vector
        def _(dve):
            steps = [0]

            def step(ins):
                ins.then_inc(dve_step, 1)
                steps[0] += 1
                dve.wait_ge(dve_step, steps[0])

            nc.vector.memset(ones[:, :], 1.0).then_inc(ones_ok, 1)
            nc.vector.memset(u[:, 0:CONV_TAPS - 1], 0.0).then_inc(ones_ok, 1)

            def sum_chunk(j, total):
                dve.wait_ge(ada_in[j % 3], 32 * (j // 3 + 1))
                for r in range(R):
                    src = ada[:, j % 3, :, r, :]
                    if r == 0:
                        ins = nc.vector.tensor_scalar(total, src, sc[:, 0:1], None, ALU.mult)
                    else:
                        dve.wait_ge(chain, R * j + r)
                        ins = nc.vector.scalar_tensor_tensor(out=total, in0=src, scalar=sc[:, r:r + 1],
                                                             in1=total, op0=ALU.mult, op1=ALU.add)
                    ins.then_inc(chain, 1)

            def modulation(j):
                dve.wait_ge(mod_sum, j + 1)
                nc.vector.tensor_scalar(gs[:, j:j + 1], bank(7, 2 * j, 2 * j + 1), b1[:, j:j + 1], prmT[:, 24 + j:25 + j],
                                        ALU.add, ALU.mult).then_inc(mod_ok, 1)
                nc.vector.tensor_scalar(sh[:, j:j + 1], bank(7, 2 * j + 1, 2 * j + 2), prmT[:, j:j + 1], None,
                                        ALU.add).then_inc(mod_ok, 1)
                dve.wait_ge(mod_ok, 2 * j + 2)
                dve.wait_ge(x_tr, j + 1)
                if j >= 2:
                    dve.wait_ge(hlo_ok, j - 1)
                nc.vector.tensor_scalar(h32[:, j % 2], bank(6), gs[:, j:j + 1], sh[:, j:j + 1],
                                        ALU.mult, ALU.add).then_inc(h_ok, 1)

            dve.wait_ge(pos_in, 32)
            nc.vector.tensor_copy(posf[0:TT, :], posi[0:TT, :]).then_inc(posf_ok, 1)
            dve.wait_ge(pos_tr, 1)
            step(nc.vector.tensor_copy(posT[:, :], bank(7, 128, 128 + TT)))
            for m in range(TT):
                ins = nc.vector.tensor_scalar(ang[:, m, :], invf[:, :], posT[:, m:m + 1], None, ALU.mult)
            step(ins)
            step(nc.vector.tensor_scalar(turns[:, :, :], ang[:, :, :], TWO_PI_INV, ROUND, ALU.mult, ALU.add))
            step(nc.vector.tensor_scalar(turns[:, :, :], turns[:, :, :], ROUND, None, ALU.subtract))
            for piece in two_pi_pieces(4, 2.0 ** -45):
                step(nc.vector.scalar_tensor_tensor(out=ang[:, :, :], in0=turns[:, :, :], scalar=-piece,
                                                    in1=ang[:, :, :], op0=ALU.mult, op1=ALU.add))
            step(nc.vector.tensor_scalar(ang[:, :, :], ang[:, :, :], PI_BELOW, -PI_BELOW, ALU.min, ALU.max))
            step(nc.vector.scalar_tensor_tensor(out=turns[:, :, :], in0=ang[:, :, :], scalar=-1.0, in1=ang[:, :, :],
                                                op0=ALU.mult, op1=ALU.min))
            nc.vector.tensor_scalar(turns[:, :, :], turns[:, :, :], PI / 2, None, ALU.add).then_inc(angle_ok, 1)

            for m in range(TT):
                dve.wait_ge(x_rstd, m + 1)
                nc.vector.tensor_scalar(xt[:, m, :], xt[:, m, :], small[:, 16 + m:17 + m], None,
                                        ALU.mult).then_inc(x_norm, 1)
            dve.wait_ge(prm_tr, 1)
            step(nc.vector.tensor_copy(prmT[:, 0:52], bank(7, 64, 64 + 52)))
            nc.vector.tensor_scalar(b1[:, :], prmT[:, 8:16], 1.0, None, ALU.add).then_inc(prm_ok, 1)
            dve.wait_ge(silu_c, 1)
            sum_chunk(0, acc[:, 0])
            dve.wait_ge(prm_ok, 1)
            for j in range(KT):
                modulation(j)
                if j + 1 < KT:
                    if j + 1 >= 2:
                        dve.wait_ge(mod_sum, j)
                    sum_chunk(j + 1, acc[:, (j + 1) % 2])

            for i in range(GC):
                sum_chunk(KT + i, gate_acc[:, i].rearrange("p (a n) -> p a n", n=P))
            dve.wait_ge(gate_in, 16)
            for i in range(GC):
                dve.wait_ge(gate_sum, i + 1)
                gg = gate[:, i * 256:(i + 1) * 256]
                nc.vector.tensor_tensor(gg, gg, ps[:, 6 * BANK + i * 256:6 * BANK + (i + 1) * 256], ALU.add
                                        ).then_inc(gate_ok, 1)

            def rope_part(p, part, to, count):
                if isinstance(p, int):
                    raw = qkv[:, p, part, :]
                else:
                    raw = qkv[:, bass.ds(p, 1), part, :].rearrange("p a n -> p (a n)")
                raw = raw.rearrange("p (m h f) -> p m h f", h=2, f=HEAD_DIM)
                m1 = rope_m[:, 0].rearrange("p m (h f) -> p m h f", h=2)
                m2 = rope_m[:, 1].rearrange("p m (h f) -> p m h f", h=2)
                o = to.rearrange("p m (h f) -> p m h f", h=2)
                for h in range(2):
                    nc.vector.tensor_tensor(m1[:, :, h], raw[:, :, h], cos_t[:, :, :], ALU.mult)
                    ins = nc.vector.tensor_tensor(m2[:, :, h], raw[:, :, h], sin_t[:, :, :], ALU.mult)
                ins.then_inc(rope_ok, 1)
                dve.wait_ge(rope_ok, count)
                m1, m2 = (t.rearrange("p m (h f) -> p (m h) f", h=2) for t in (rope_m[:, 0], rope_m[:, 1]))
                o = to.rearrange("p m (h f) -> p (m h) f", h=2)
                nc.vector.tensor_tensor(o[:, :, 0:HALF], m1[:, :, 0:HALF], m2[:, :, HALF:], ALU.subtract)
                nc.vector.tensor_tensor(o[:, :, HALF:], m1[:, :, HALF:], m2[:, :, 0:HALF], ALU.add).then_inc(rope_ok, 1)

            def rope_pair(p, count):
                rope_part(p, 0, rope_q, count + 1)
                dve.wait_ge(rope_ok, count + 2)
                rope_part(p, 1, rope_k, count + 3)

            dve.wait_ge(trig_ok, 4)
            dve.wait_ge(qkv_evac, 2 * TT)
            rope_pair(0, 0)

            def least(p, head):
                for n, i in enumerate(S_ORDER):
                    if n != 1:
                        count = p * 6 + (3 * head + max(n, 1))
                        if not isinstance(p, int):
                            dve.to_reg(count)
                        dve.wait_ge(mask_ok, 1)
                        dve.wait_ge(scores, count)
                    a, w = S_AT[i], P * (i + 1)
                    e = 4 * head + n
                    dve.tensor_tensor_reduce(probs[:, a:a + w], mask[:, S - w:S], ps[:, SB + a:SB + a + w], 1.0,
                                             3.0e38, ALU.add, ALU.min, rmin[:, e:e + 1]).then_inc(row_min, 1)

            def normalise(p, head, count):
                dve.wait_ge(exps, p * 8 + (4 * head + 4))
                nc.vector.reciprocal(prec[:, 4 * head:4 * head + 4], psums[:, 4 * head:4 * head + 4]).then_inc(p_norm, 1)
                dve.wait_ge(p_norm, p * 4 + (2 * head + 1))
                for n, i in enumerate(S_ORDER):
                    a, w = S_AT[i], P * (i + 1)
                    e = 4 * head + n
                    ins = nc.vector.tensor_scalar(probs[:, a:a + w], probs[:, a:a + w], prec[:, e:e + 1], None, ALU.mult)
                ins.then_inc(p_norm, 1)

            def low_probs(p, head):
                dve.wait_ge(p_hi, p * 2 + (head + 1))
                nc.vector.tensor_tensor(pt_lo[:, :], ps[:, TB:TB + TRI], pt_hi[:, :].bitcast(F32), ALU.subtract
                                        ).then_inc(p_lo, 1)

            dve.wait_ge(mask_ok, 1)

            def column(p, row, last):
                return prmT[:, row + p:row + p + 1] if last else prmT[:, bass.ds(p + row, 1)]

            def turn(p, last):
                dve.wait_ge(c_copy, p + 1)
                dve.wait_ge(tile_out, p * NT + 2)
                nc.vector.tensor_tensor(u[:, CONV_TAPS - 1:], cz[:, :], bank(H_BANK), ALU.mult).then_inc(u_ok, 1)
                dve.wait_ge(qk_hi, p * 6 + 2)
                for head in range(2):
                    a, b = head * 64, head * 64 + 64
                    o = (1 - head) * 64
                    nc.vector.scalar_tensor_tensor(out=qs[o:o + 64, head, :], in0=bank(Q_BANK, p0=a, p1=b),
                                                   scalar=-(HEAD_DIM ** -0.5), in1=qs[a:b, head, :].bitcast(F32),
                                                   op0=ALU.mult, op1=ALU.subtract)
                    if head == 0:
                        dve.wait_ge(qk_hi, p * 6 + 6)
                    for to in range(2):
                        ins = nc.vector.tensor_tensor(k_lo[to * 64:to * 64 + 64, head, :], bank(K_BANK, p0=a, p1=b),
                                                      k_hi[a:b, head, :].bitcast(F32), ALU.subtract)
                    ins.then_inc(qk_split, 1)
                dve.wait_ge(u_ok, p + 1)
                for tap in range(CONV_TAPS):
                    wc = column(p, 40 + NP * tap, last)
                    if tap == 0:
                        nc.vector.tensor_scalar(yc[:, :], u[:, 0:S], wc, None, ALU.mult).then_inc(tap_ok, 1)
                    else:
                        nc.vector.scalar_tensor_tensor(out=yc[:, :], in0=u[:, tap:tap + S], scalar=wc, in1=yc[:, :],
                                                       op0=ALU.mult, op1=ALU.add).then_inc(tap_ok, 1)
                    dve.wait_ge(tap_ok, p * 3 + (tap + 1))
                least(p, 0)
                dve.wait_ge(tile_out, p * NT + (B_ + 3))
                nc.vector.tensor_tensor(yc[:, :], yc[:, :], bank(TILE_BANK[B_]), ALU.mult).then_inc(y_conv, 1)
                normalise(p, 0, 0)
                least(p, 1)
                low_probs(p, 0)
                normalise(p, 1, 0)
                dve.wait_ge(bank1_free, p + 2)
                dve.wait_ge(v_lo, p * 2 + 2)
                dve.wait_ge(y_conv, p + 1)
                nc.vector.scalar_tensor_tensor(out=yg[:, :], in0=yc[:, :], scalar=column(p, 36, last), in1=cz[:, :],
                                               op0=ALU.mult, op1=ALU.mult).then_inc(y_gated, 1)
                if not last:
                    rope_part(p + 1, 0, rope_q, p * 4 + 5)
                dve.wait_ge(y_tmp, p * 2 + 1)
                nc.vector.tensor_tensor(ya[0:64, :], ytmp[0:64, :], bank(2, p0=0, p1=64), ALU.add).then_inc(y_attn, 1)
                low_probs(p, 1)
                if not last:
                    dve.wait_ge(rope_ok, p * 4 + 6)
                    rope_part(p + 1, 1, rope_k, p * 4 + 7)
                dve.wait_ge(y_tmp, p * 2 + 2)
                nc.vector.tensor_tensor(ya[64:128, :], ytmp[64:128, :], bank(3, p0=64, p1=128), ALU.add
                                        ).then_inc(y_attn, 1)
                dve.wait_ge(bank0_free, p + 2)
                dve.wait_ge(y_lo, p * 2 + 1)
                dve.wait_ge(y_attn, p * 2 + 2)
                nc.vector.scalar_tensor_tensor(out=yg[:, :], in0=ya[:, :], scalar=column(p, 32, last), in1=za[:, :],
                                               op0=ALU.mult, op1=ALU.mult).then_inc(y_gated, 1)

            with dve.Fori(0, NP - 1) as p:
                turn(p, False)
            turn(NP - 1, True)

            dve.wait_ge(ssq_out, 1)
            nc.vector.tensor_scalar(small[:, 40:48], bank(7, 0, 8), 1.0 / DA, EPS, ALU.mult, ALU.add
                                    ).then_inc(ssq_ok, 1)
            dve.wait_ge(gate_ok, 4)
            dve.wait_ge(x2_in, 16 * TT)
            dve.wait_ge(rs_ok, 1)

            def add_conv(n, m):
                cols = slice(n * BANK, (n + 1) * BANK)
                dve.wait_ge(conv_evac, n * TT + m + 1)
                step(nc.vector.tensor_tensor(oc[:, m], oc[:, m], gate[:, cols], ALU.mult))
                nc.vector.tensor_tensor(x2[:, m, cols], x2[:, m, cols], oc[:, m], ALU.add).then_inc(conv_added, 1)

            def add_attn(n, m):
                cols = slice(n * BANK, (n + 1) * BANK)
                dve.wait_ge(attn_out, n * TT + m + 1)
                nc.vector.scalar_tensor_tensor(out=om[:, m % 2], in0=bank(ATTN_BANK[m]), scalar=rs[:, TT + m:TT + m + 1],
                                               in1=gate[:, cols], op0=ALU.mult, op1=ALU.mult).then_inc(attn_evac, 1)
                dve.wait_ge(conv_added, n * TT + m + 1)
                dve.wait_ge(attn_evac, n * TT + m + 1)
                nc.vector.tensor_tensor(x2[:, m, cols], x2[:, m, cols], om[:, m % 2], ALU.add).then_inc(x2_ok, 1)

            def scale_right(m):
                dve.wait_ge(fin_rs, m + 1)
                nc.vector.scalar_tensor_tensor(out=x2[:, m, BANK:], in0=x2[:, m, BANK:], scalar=small[:, 56 + m:57 + m],
                                               in1=gfin[:, BANK:], op0=ALU.mult, op1=ALU.mult).then_inc(fin_right, 1)

            for n in range(2):
                for m in range(TT):
                    add_conv(n, m)
                for m in range(TT):
                    add_attn(n, m)
                    if n and m:
                        scale_right(m - 1)
            scale_right(TT - 1)

        @block.tensor
        def _(pe):
            def mm3(o, a_hi, a_lo, b_hi, b_lo, start, stop):
                nc.tensor.matmul(o, a_hi, b_lo, start=start, stop=False)
                nc.tensor.matmul(o, a_lo, b_hi, start=False, stop=False)
                return nc.tensor.matmul(o, a_hi, b_hi, start=False, stop=stop)

            pe.wait_ge(ident_ok, 1)
            pe.wait_ge(posf_ok, 1)
            nc.tensor.transpose(bank(7, 128, 128 + TT), posf[0:TT, :], ident[0:TT, 0:TT]).then_inc(pos_tr, 1)
            pe.wait_ge(ones_ok, 1)

            def x_tile(j):
                if j:
                    pe.wait_ge(h_ok, j)
                for m in range(TT):
                    if j == 0:
                        pe.wait_ge(x_norm, m + 1)
                    ins = nc.tensor.transpose(bank(6, m * P, (m + 1) * P), xt[:, m, j * P:(j + 1) * P], ident[:, :])
                ins.then_inc(x_tr, 1)

            def mod_tile(j):
                pe.wait_ge(chain, R * (j + 1))
                for two in range(2):
                    ins = nc.tensor.matmul(bank(7, 2 * j + two, 2 * j + two + 1), acc[:, j % 2, two, :], ones[:, 0:1],
                                           start=True, stop=True)
                ins.then_inc(mod_sum, 1)

            def slab(g, k):
                for m in range(TT):
                    if not isinstance(g, int) and k == 0:
                        pe.wait_ge(qkv_evac, g * TT + (m + 1 - TT))
                    t = slice(m * P, (m + 1) * P)
                    ins = mm3(bank(m), h_hi[:, k, t], h_lo[:, k, t], w_hi[:, k, :], w_lo[:, k, :], k == 0, k == KT - 1)
                    if k == KT - 1:
                        ins.then_inc(qkv_out, 1)
                if k < KT - 1:
                    ins.then_inc(slab_used, 1)

            x_tile(0)
            pe.wait_ge(prm_in, 16 * 5)
            pe.wait_ge(angle_ok, 1)
            nc.tensor.transpose(bank(7, 64, 64 + 52), prm[0:52, :], ident[0:52, 0:52]).then_inc(prm_tr, 1)
            mod_tile(0)
            for j in range(KT):
                pe.wait_ge(slab_lo, j + 1)
                pe.wait_ge(hlo_ok, j + 1)
                for two, b in ((0, C_BANK), (1, H_BANK)):
                    ins = mm3(bank(b), ch_hi[:, j % 2, two], ch_lo[:, j % 2, two], h_hi[:, j], h_lo[:, j],
                              j == 0, j == KT - 1)
                    if j == KT - 1:
                        ins.then_inc(tile_out, 1)
                if j < KT - 1:
                    ins.then_inc(ch_used, 1)
                if j + 1 < KT:
                    x_tile(j + 1)
                    mod_tile(j + 1)
                slab(0, j)

            with pe.Fori(1, 3) as g:
                for k in range(KT):
                    pe.wait_ge(slab_lo, g * KT + (k + 1))
                    slab(g, k)
                    if k in (3, 4):
                        i = k - 3
                        pe.wait_ge(chain, g * (2 * R) + (R * KT - 2 * R + (i + 1) * R))
                        if i:
                            pe.wait_ge(gate_ok, g * 2 - 1)
                        nc.tensor.matmul(ps[:, bass.ds(g * 512 + (6 * BANK - 512 + i * 256), 256)], ones[:, :],
                                         gate_acc[:, bass.ds(g * 2 + (i - 2), 1)].rearrange("p a n -> p (a n)"),
                                         start=True, stop=True).then_inc(gate_sum, 1)

            BANK_FREE = [bank0_free, bank1_free, y_conv, None, None]

            def tile(p, t):
                pe.wait_ge(tile_lo, p * NT + (t + 1))
                if BANK_FREE[t]:
                    pe.wait_ge(BANK_FREE[t], p + 1)
                for k in range(KT):
                    ins = mm3(bank(TILE_BANK[t]), t_hi[:, t, k], t_lo[:, t, k], h_hi[:, k], h_lo[:, k],
                              k == 0, k == KT - 1)
                ins.then_inc(tile_out, 1)

            def score(p, head):
                for n, i in enumerate(S_ORDER):
                    o = ps[:, SB + S_AT[i]:SB + S_AT[i] + P * (i + 1)]
                    q = qs[:, head, i * P:(i + 1) * P]
                    nc.tensor.matmul(o, q, k_lo[:, head, 0:P * (i + 1)], start=True, stop=False)
                    ins = nc.tensor.matmul(o, q, k_hi[:, head, 0:P * (i + 1)], start=False, stop=True)
                    if n:
                        ins.then_inc(scores, 1)

            def transpose_probs():
                for i in range(TT):
                    for j in range(i + 1):
                        a = S_AT[i] + j * P
                        o = TB + T_AT[j] + (i - j) * P
                        ins = nc.tensor.transpose(ps[:, o:o + P], probs[:, a:a + P], ident[:, :])
                ins.then_inc(p_tr, 1)

            def values(head):
                for j in range(TT):
                    for n, pt in enumerate((pt_lo, pt_hi)):
                        ins = nc.tensor.matmul(bank(2 + head, j * P, BANK), v2[:, head, j, :],
                                               pt[:, T_AT[j]:T_AT[j] + S - j * P],
                                               start=(j == 0 and n == 0), stop=(j == TT - 1 and n == 1))
                ins.then_inc(pv_out, 1)

            def project(n, part, m, b, rows):
                t = slice(m * P, (m + 1) * P)
                for k in range(NP):
                    ins = mm3(bank(b), y[:, k, part, t], y[:, k, part + 1, t], w_hi[:, rows + k], w_lo[:, rows + k],
                              k == 0, k == NP - 1)
                return ins

            def turn(p, last):
                for n, (src, b) in enumerate(((rope_q, Q_BANK), (rope_k, K_BANK))):
                    pe.wait_ge(rope_ok, p * 4 + (2 * n + 2))
                    if n == 0:
                        pe.wait_ge(gate_ok, GC)
                    for m in range(TT):
                        ins = nc.tensor.transpose(bank(b, m * P, (m + 1) * P), src[:, m, :], ident[:, :])
                    ins.then_inc(qk_tr, 1)
                tile(p, B_)
                pe.wait_ge(qk_split, p * 2 + 1)
                score(p, 0)
                tile(p, ZC)
                pe.wait_ge(p_norm, p * 4 + 2)
                transpose_probs()
                pe.wait_ge(qk_split, p * 2 + 2)
                score(p, 1)
                tile(p, ZA)
                pe.wait_ge(p_lo, p * 2 + 1)
                pe.wait_ge(v_lo, p * 2 + 2)
                pe.wait_ge(row_min, p * 8 + 8)
                values(0)
                pe.wait_ge(p_norm, p * 4 + 4)
                transpose_probs()
                if last:
                    pe.wait_ge(slab_lo, 4 * KT)
                    pe.wait_ge(y_lo, 2 * NP - 1)
                    pe.wait_ge(bank1_free, NP + 1)
                    for m in range(2):
                        project(0, 2, m, CONV_BANK[m], NP).then_inc(conv_out, 1)
                else:
                    tile(p, CN)
                pe.wait_ge(p_lo, p * 2 + 2)
                values(1)
                if not last:
                    tile(p, HN)

            with pe.Fori(0, NP - 1) as p:
                turn(p, False)
            turn(NP - 1, True)

            pe.wait_ge(bank0_free, NP + 1)
            pe.wait_ge(y_attn, 2 * NP - 1)
            for m in (2, 3):
                project(0, 2, m, CONV_BANK[m], NP).then_inc(conv_out, 1)
            pe.wait_ge(y_attn, 2 * NP)
            pe.wait_ge(y_lo, 2 * NP)
            for m in range(TT):
                if m == 2:
                    pe.wait_ge(sq_added, 2 * NP + 1)
                    for part in range(2):
                        for i in range(TT):
                            ins = nc.tensor.matmul(bank(7, part * TT + i, part * TT + i + 1),
                                                   sqsum[:, part, i * P:(i + 1) * P], ones[:, 0:1], start=True, stop=True)
                    ins.then_inc(ssq_out, 1)
                if m == 3:
                    pe.wait_ge(ssq_ok, 1)
                project(0, 0, m, ATTN_BANK[m], 0).then_inc(attn_out, 1)
            pe.wait_ge(slab_lo, 4 * KT + 4)
            for m in range(TT):
                pe.wait_ge(conv_evac, m + 1)
                project(1, 2, m, CONV_BANK[m], NP).then_inc(conv_out, 1)
            pe.wait_ge(slab_lo, 5 * KT)
            for m in range(TT):
                pe.wait_ge(attn_evac, m + 1)
                project(1, 0, m, ATTN_BANK[m], 0).then_inc(attn_out, 1)


_INS = ["x", "c", "positions", "w_ada", "b_ada", "g_norm", "w_in", "w_conv", "g_attn_out", "g_conv_out",
        "w_out", "g_final"]


def kernel(**inputs):
    import numpy as np
    import concourse.bacc as bacc
    from concourse.bass_utils import run_bass_kernel_spmd as run

    nc = bacc.Bacc("TRN2", target_bir_lowering=False, num_devices=1, dynamic_dma_scratch_size=64)
    arrays, args = {}, []
    given = [(name, np.ascontiguousarray(inputs[name])) for name in _INS]
    half = HEAD_DIM // 2
    given.append(("inv_freq", (10000.0 ** (-np.arange(half) / half)).astype(np.float32)))
    for name, a in given:
        arrays[f"in_{name}"] = a
        args.append(nc.dram_tensor(f"in_{name}", a.shape, mybir.dt.from_np(a.dtype), kind="ExternalInput").ap())
    shape = inputs["x"].shape
    args.append(nc.dram_tensor("out_0", shape, F32, kind="ExternalOutput").ap())
    build(nc, *args)
    r = run(nc, [arrays], core_ids=[0])
    return r.results[0]["out_0"]
```

```python
from contextlib import ExitStack

import concourse.bass as bass
from concourse import mybir

F32 = mybir.dt.float32
F32R = mybir.dt.float32r
I32 = mybir.dt.int32
ALU = mybir.AluOpType
ACT = mybir.ActivationFunctionType

P = 128
BANK = 512
HEAD_DIM = 64
CONV_TAPS = 3
EPS = 1e-6
MASKED = 1e30
PI = 3.141592653589793
TWO_PI_INV = 1.0 / (2.0 * PI)
ROUND = 1.5 * 2.0 ** 23
PI_BELOW = 3.1415925


def two_pi_pieces(bits, low):
    pieces, rest, unit = [], 2.0 * PI, 2.0 ** (3 - bits)
    while unit >= low:
        piece = int(rest / unit) * unit
        if piece:
            pieces.append(piece)
        rest -= piece
        unit /= 2.0 ** bits
    return pieces


def build(nc, x, c, positions, w_ada, b_ada, g_norm, w_in, w_conv, g_attn_out, g_conv_out,
          w_out, g_final, inv_freq, out):
    _, S, D = x.shape
    DA = g_attn_out.shape[0]
    KT = D // P
    TT = S // P
    NP = DA // P
    HALF = HEAD_DIM // 2
    R = D // P
    RV = 6
    GC = D // 256
    assert S == BANK and KT == 8 and TT == 4 and NP == 4 and D == 2 * BANK

    B_, ZC, ZA, CN, HN = range(5)
    COLS = [4 * DA, 7 * DA, 3 * DA, 5 * DA, 6 * DA]
    NT = len(COLS)
    TILE_BANK = [0, 1, 0, 4, 5]
    RAW_SLOT = [0, 1, 2, 0, 1]
    C_BANK, H_BANK = TILE_BANK[CN], TILE_BANK[HN]
    Q_BANK, K_BANK = 6, 7
    CONV_BANK, ATTN_BANK = [1, 4, 0, 2], [5, 6, 3, 7]
    PIECES = [(n, m, 0, BANK, ATTN_BANK[m]) for n in range(2) for m in range(TT)][:-1]
    PIECES += [(1, TT - 1, 0, BANK // 2, ATTN_BANK[TT - 1]), (1, TT - 1, BANK // 2, BANK, CONV_BANK[0])]

    S_AT = {3: 0, 2: 512, 0: 896, 1: 1024}
    T_AT = {0: 0, 1: 512, 3: 896, 2: 1024}
    S_ORDER = [2, 0, 3, 1]
    TRI = 1280
    SB, TB = 2 * BANK, 5 * BANK

    with ExitStack() as ctx:
        cursor = [(nc.sbuf_base + 31) // 32 * 32]

        def at(name, offset, shape, dt=F32):
            return nc.alloc_sbuf_tensor_at(name, [P, *shape], dt, offset=offset)

        def sb(name, shape, dt=F32):
            size = 4
            for n in shape:
                size *= n
            offset = cursor[0]
            cursor[0] = (offset + size + 31) // 32 * 32
            return at(name, offset, shape, dt)

        def sem(name):
            return ctx.enter_context(nc.semaphore(name))

        h_hi = sb("h_hi", [KT, S], F32R)
        h_lo = sb("h_lo", [KT, S], F32R)
        w_hi = sb("w_hi", [8, BANK], F32R)
        w_lo = sb("w_lo", [8, BANK], F32R)
        w_raw = sb("w_raw", [4, BANK])
        tile_raw = sb("tile_raw", [3, KT, P])
        rope_q = sb("rope_q", [TT, P])
        rope_k = sb("rope_k", [TT, P])
        cos_t = sb("cos_t", [TT, HEAD_DIM])
        sin_t = sb("sin_t", [TT, HEAD_DIM])
        rope_m = sb("rope_m", [2, TT, P])
        ch_hi = at("ch_hi", cursor[0], [2, 2, P], F32R)
        qs = sb("qs", [2, S], F32R)
        ch_lo = at("ch_lo", cursor[0], [2, 2, P], F32R)
        k_hi = sb("k_hi", [2, S], F32R)
        ch_raw = at("ch_raw", cursor[0], [4, 2, P])
        k_lo = sb("k_lo", [2, S], F32R)
        pt_hi = sb("pt_hi", [TRI], F32R)
        gate_acc = at("gate_acc", cursor[0], [GC, 256])
        pt_lo = sb("pt_lo", [TRI], F32R)
        v2 = sb("v2", [2, TT, P], F32R)
        cz = sb("cz", [S])
        u = sb("u", [S + CONV_TAPS - 1])
        yc = sb("yc", [S])
        invf = at("invf", cursor[0], [HALF])
        ang = at("ang", cursor[0] + 4 * HALF, [TT, HALF])
        turns = at("turns", cursor[0] + 4 * HALF * (TT + 1), [TT, HALF])
        yg = sb("yg", [S])
        ya = sb("ya", [S])
        za = sb("za", [S])
        ytmp = at("ytmp", cursor[0], [S])
        sq = sb("sq", [S])
        sqsum = sb("sqsum", [2, S])
        mask = sb("mask", [S])
        probs = sb("probs", [TRI])
        ident = sb("ident", [P])
        ones = sb("ones", [P])
        gate = sb("gate", [D])
        prmT = sb("prmT", [64])
        cs = sb("cs", [R])
        sc = sb("sc", [R])
        gs = sb("gs", [KT])
        sh = sb("sh", [KT])
        b1 = sb("b1", [KT])
        small = sb("small", [64])
        rmin = sb("rmin", [8])
        psums = sb("psums", [8])
        prec = sb("prec", [8])
        rs = sb("rs", [8])
        ss2 = sb("ss2", [16])
        posT = sb("posT", [TT])
        base = cursor[0]
        sb("y_", [NP, 4, S])
        xt = at("xt", base, [TT, D])
        qkv = at("qkv", base, [NP, 4, S])
        y = at("y", base, [NP, 4, S], F32R)
        base = cursor[0]
        sb("tile_", [2 * NT, KT * P])
        t_hi = at("t_hi", base, [NT, KT, P], F32R)
        t_lo = at("t_lo", base + NT * KT * P * 4, [NT, KT, P], F32R)
        ada = at("ada", base, [3, 2, R, P])
        acc = at("acc", base + 24576, [2, 2, P])
        prod = at("prod", base + 26624, [2, 2, P])
        prod_sum = at("prod_sum", base + 28672, [2, P])
        h32 = at("h32", base + 30720, [2, S])
        junk = at("junk", base + 34816, [D])
        x2 = at("x2", base, [TT, D])
        gfin = at("gfin", base + 16384, [D])
        oc = at("oc", base + 20480, [TT, BANK])
        om = at("om", base + 28672, [2, BANK])
        junk2 = at("junk2", base + 32768, [BANK])
        prm = at("prm", base + 38912, [P])
        posi = at("posi", base + 39424, [P], I32)
        posf = at("posf", base + 39936, [P])
        assert cursor[0] <= nc.sbuf_usable_end, (cursor[0], nc.sbuf_usable_end)

        ps = ctx.enter_context(nc.psum_tensor("ps", [P, 8 * BANK], F32))

        def bank(b, lo=0, hi=BANK, p0=0, p1=P):
            return ps[p0:p1, b * BANK + lo:b * BANK + hi]

        c_in, pos_in, prm_in, gate_in = sem("c_in"), sem("pos_in"), sem("prm_in"), sem("gate_in")
        x_in = [sem(f"x_in{m}") for m in range(TT)]
        ada_in = [sem(f"ada_in{i}") for i in range(3)]
        raw_in = [sem(f"raw_in{i}") for i in range(4)]
        ch_in = [sem(f"ch_in{i}") for i in range(4)]
        tile_in = [sem(f"tile_in{i}") for i in range(3)]
        x2_in, gfin_in, out_done = sem("x2_in"), sem("gfin_in"), sem("out_done")
        ident_ok, mask_ok, ones_ok, pool_step = sem("ident_ok"), sem("mask_ok"), sem("ones_ok"), sem("pool_step")
        silu_c, x_sq, x_rstd, x_norm = sem("silu_c"), sem("x_sq"), sem("x_rstd"), sem("x_norm")
        prm_tr, pos_tr, prm_ok, posf_ok = sem("prm_tr"), sem("pos_tr"), sem("prm_ok"), sem("posf_ok")
        prods, prods_added = sem("prods"), sem("prods_added")
        chain, mod_sum, mod_ok = sem("chain"), sem("mod_sum"), sem("mod_ok")
        x_tr, h_ok, hhi_ok, hlo_ok = sem("x_tr"), sem("h_ok"), sem("hhi_ok"), sem("hlo_ok")
        slab_hi, slab_lo, slab_used, ch_used = sem("slab_hi"), sem("slab_lo"), sem("slab_used"), sem("ch_used")
        qkv_out, qkv_evac, gate_sum, gate_ok = sem("qkv_out"), sem("qkv_evac"), sem("gate_sum"), sem("gate_ok")
        dve_step, angle, pos_read = sem("dve_step"), sem("angle"), sem("pos_read")
        trig_ok, rope_ok = sem("trig_ok"), sem("rope_ok")
        tile_hi, tile_lo, tile_out = sem("tile_hi"), sem("tile_lo"), sem("tile_out")
        bank0_free, bank1_free, u_ok, tap_ok = sem("bank0_free"), sem("bank1_free"), sem("u_ok"), sem("tap_ok")
        qk_tr, qk_hi, qk_split, v_hi, v_lo = sem("qk_tr"), sem("qk_hi"), sem("qk_split"), sem("v_hi"), sem("v_lo")
        scores, row_min, exps, p_norm = sem("scores"), sem("row_min"), sem("exps"), sem("p_norm")
        p_tr, p_hi, p_lo, pv_out = sem("p_tr"), sem("p_hi"), sem("p_lo"), sem("pv_out")
        y_tmp, y_attn, c_copy, y_conv = sem("y_tmp"), sem("y_attn"), sem("c_copy"), sem("y_conv")
        y_gated, y_hi, y_lo = sem("y_gated"), sem("y_hi"), sem("y_lo")
        sq_ok, sq_added = sem("sq_ok"), sem("sq_added")
        ssq_out, ssq_ok, rs_ok = sem("ssq_out"), sem("ssq_ok"), sem("rs_ok")
        conv_out, attn_out, conv_evac, attn_evac = sem("conv_out"), sem("attn_out"), sem("conv_evac"), sem("attn_evac")
        conv_added = sem("conv_added")
        x2_ok, x2_sq, x2_g, ss2_eps, fin_rs = sem("x2_ok"), sem("x2_sq"), sem("x2_g"), sem("ss2_eps"), sem("fin_rs")
        fin_left, fin_right = sem("fin_left"), sem("fin_right")

        angle_steps = 1 + 5 + len(two_pi_pieces(4, 2.0 ** -45))

        w_ada_v = w_ada.rearrange("(p r) n -> p r n", r=R)
        w_in_v = w_in.rearrange("(k p) n -> k p n", p=P)
        w_in_t = w_in.rearrange("(k p) n -> p k n", p=P)
        w_out_v = w_out.rearrange("(k p) n -> k p n", p=P)

        def chained(j):
            return R * j - (R - RV) * max(0, min(j, KT) - 2)

        block = ctx.enter_context(nc.Block())

        @block.sync
        def _(sp):
            def ada_chunk(j):
                for two in range(2):
                    col = (1 - two) * D + j * P if j < KT else 2 * D + (2 * (j - KT) + two) * P
                    sp.dma_start(ada[:, j % 3, two], w_ada_v[:, :, col:col + P]).then_inc(ada_in[j % 3], 16)

            ada_chunk(0)
            sp.dma_start(cs[:, :], c.rearrange("a (p r) -> p (a r)", r=R)).then_inc(c_in, 16)
            sp.dma_start(posi[0:TT, :], positions.rearrange("a (t p) -> (a t) p", p=P)).then_inc(pos_in, 16)
            sp.dma_start(invf[:, :], inv_freq.partition_broadcast(P)).then_inc(pos_in, 16)
            for m in range(TT):
                sp.dma_start(xt[:, m, :], x[0, m * P:(m + 1) * P, :]).then_inc(x_in[m], 16)
            row = 0
            for src in (b_ada.rearrange("(t p) -> t p", p=P), g_norm.rearrange("(t p) -> t p", p=P),
                        g_attn_out.rearrange("(t p) -> t p", p=P), g_conv_out.rearrange("(t p) -> t p", p=P),
                        w_conv.rearrange("a (t p) -> (a t) p", p=P)):
                n = src.shape[0]
                sp.dma_start(prm[row:row + n, :], src).then_inc(prm_in, 16)
                row += n
            for j in range(KT):
                if j:
                    if j >= 3:
                        sp.wait_ge(chain, chained(j - 2))
                    ada_chunk(j)
                if j >= 4:
                    sp.wait_ge(slab_lo, j - 3)
                sp.dma_start(w_raw[:, j % 4], w_in_v[j, :, 0:BANK]).then_inc(raw_in[j % 4], 16)
                sp.dma_start(ch_raw[:, j % 4],
                             w_in_v[j, :, COLS[CN]:COLS[CN] + 2 * DA].rearrange("p (two n) -> p two n", two=2)[:, :, 0:P]
                             ).then_inc(ch_in[j % 4], 16)
            for k in range(KT):
                sp.wait_ge(slab_lo, KT + k - 3)
                sp.dma_start(w_raw[:, k % 4], w_in_v[k, :, BANK:2 * BANK]).then_inc(raw_in[k % 4], 16)
                if k % 2 == 0:
                    sp.wait_ge(chain, chained(KT + k // 2 - 2))
                    ada_chunk(KT + k // 2)
            sp.dma_start(gate[:, :], b_ada[2 * D:3 * D].partition_broadcast(P)).then_inc(gate_in, 16)
            for t in (B_, ZC, ZA):
                sp.dma_start(tile_raw[:, RAW_SLOT[t]], w_in_t[:, :, COLS[t]:COLS[t] + P]
                             ).then_inc(tile_in[RAW_SLOT[t]], 16)
            for k in range(KT):
                sp.wait_ge(slab_lo, 2 * KT + k - 3)
                sp.dma_start(w_raw[:, k % 4], w_in_v[k, :, 2 * BANK:3 * BANK]).then_inc(raw_in[k % 4], 16)

            def turn(p, last):
                for i in range(2):
                    sp.wait_ge(slab_lo, p * 2 + 3 * KT)
                    sp.dma_start(w_raw[:, i], w_out_v[bass.ds(p * 2 + i, 1), :, 0:BANK].rearrange("a p n -> p (a n)")
                                 ).then_inc(raw_in[i], 16)
                for n, (t, split) in enumerate([] if last else [(CN, 1), (HN, 2), (ZA, 3), (B_, 4), (ZC, 5)]):
                    sp.wait_ge(tile_lo, p * NT + split)
                    sp.dma_start(tile_raw[:, RAW_SLOT[t]],
                                 w_in_t[:, :, bass.ds(p * P + (COLS[t] + P), P)]
                                 ).then_inc(tile_in[RAW_SLOT[t]], 16)

            with sp.Fori(0, NP - 1) as p:
                turn(p, False)
            turn(NP - 1, True)
            sp.wait_ge(slab_lo, 4 * KT)
            for k in (4, 5, 6, 7):
                sp.dma_start(w_raw[:, k % 4], w_out_v[k, :, BANK:D]).then_inc(raw_in[k % 4], 16)
            sp.wait_ge(tile_out, NT * NP)
            for m in range(TT):
                sp.dma_start(x2[:, m, :], x[0, m * P:(m + 1) * P, :]).then_inc(x2_in, 16)
            sp.dma_start(gfin[:, :], g_final.partition_broadcast(P)).then_inc(gfin_in, 16)
            for k in (0, 1, 2, 3):
                sp.wait_ge(slab_lo, 4 * KT + k + 1)
                sp.dma_start(w_raw[:, k % 4], w_out_v[k, :, BANK:D]).then_inc(raw_in[k % 4], 16)
            for m in range(TT):
                sp.wait_ge(fin_left, m + 1)
                sp.wait_ge(fin_right, m + 1)
                sp.dma_start(out[0, m * P:(m + 1) * P, :], x2[:, m, :]).then_inc(out_done, 16)
            sp.wait_ge(out_done, 16 * TT)

        @block.scalar
        def _(act):
            act.wait_ge(c_in, 16)
            nc.scalar.activation(sc[:, :], cs[:, :], ACT.Silu).then_inc(silu_c, 1)
            for m in range(TT):
                act.wait_ge(x_in[m], 16)
                if m:
                    act.wait_ge(x_sq, m)
                nc.scalar.activation(junk[:, :], xt[:, m, :], ACT.Square, scale=D ** -0.5,
                                     accum_out=small[:, m:m + 1]).then_inc(x_sq, 1)

            def products(j):
                act.wait_ge(ada_in[j % 3], 32 * (j // 3 + 1))
                if j >= 3:
                    act.wait_ge(prods_added, j - 2)
                for i in range(2):
                    nc.scalar.activation(prod[:, i], ada[:, j % 3, :, RV + i, :], ACT.Copy,
                                         scale=sc[:, RV + i:RV + i + 1]).then_inc(prods, 1)

            act.wait_ge(silu_c, 1)
            for j in range(KT):
                act.wait_ge(raw_in[j % 4], 16 * (j // 4 + 1))
                nc.scalar.activation(w_hi[:, j], w_raw[:, j % 4], ACT.Copy)
                act.wait_ge(ch_in[j % 4], 16 * (j // 4 + 1))
                if j >= 2:
                    act.wait_ge(ch_used, j - 1)
                nc.scalar.activation(ch_hi[:, j % 2], ch_raw[:, j % 4], ACT.Copy).then_inc(slab_hi, 1)
                if 1 <= j < KT - 1:
                    products(j + 1)
                act.wait_ge(mod_ok, 2 * j + 2)
                act.wait_ge(x_tr, j + 1)
                if j >= 2:
                    act.wait_ge(hlo_ok, j - 1)
                nc.scalar.activation(h32[:, j % 2], bank(6), ACT.Identity, scale=gs[:, j:j + 1],
                                     bias=sh[:, j:j + 1]).then_inc(h_ok, 1)
                act.wait_ge(h_ok, j + 1)
                nc.scalar.activation(h_hi[:, j], h32[:, j % 2], ACT.Copy).then_inc(hhi_ok, 1)
                if j == KT - 1:
                    act.wait_ge(angle, angle_steps)
                    sin_v = sin_t.rearrange("p m (two f) -> p m two f", two=2)
                    cos_v = cos_t.rearrange("p m (two f) -> p m two f", two=2)
                    for two in range(2):
                        nc.scalar.activation(sin_v[:, :, two, :], ang[:, :, :], ACT.Sin).then_inc(trig_ok, 1)
                        nc.scalar.activation(cos_v[:, :, two, :], turns[:, :, :], ACT.Sin).then_inc(trig_ok, 1)
            act.wait_ge(tile_out, 1)
            nc.scalar.activation(cz[:, :], bank(C_BANK), ACT.Copy).then_inc(c_copy, 1)

            def evacuate(g, m):
                act.wait_ge(x_sq, TT)
                act.wait_ge(qkv_out, g * TT + (m + 1))
                out_ap = qkv[:, :, g, m * P:(m + 1) * P] if isinstance(g, int) else \
                    qkv[:, :, bass.ds(g, 1), m * P:(m + 1) * P].rearrange("p a g n -> p a (g n)")
                ins = nc.scalar.activation(out_ap, bank(m).rearrange("p (a n) -> p a n", n=P), ACT.Copy)
                ins.then_inc(qkv_evac, 1)

            with act.Fori(1, 3) as g:
                for k in range(KT):
                    if k == 4:
                        for m in range(TT):
                            evacuate(g - 1, m)
                    if k < KT - 1:
                        act.wait_ge(slab_used, g * (KT - 1) + (k + 1 - (KT - 1)))
                    act.wait_ge(raw_in[k % 4], g * 32 + 16 * (k // 4 + 1))
                    nc.scalar.activation(w_hi[:, k], w_raw[:, k % 4], ACT.Copy).then_inc(slab_hi, 1)
            act.wait_ge(chain, chained(KT + GC))

            def split_tile(t, arrived):
                act.wait_ge(tile_in[RAW_SLOT[t]], arrived)
                nc.scalar.activation(t_hi[:, t], tile_raw[:, RAW_SLOT[t]], ACT.Copy).then_inc(tile_hi, 1)

            for t in (B_, ZC, ZA):
                split_tile(t, 16)
            for m in range(TT):
                act.wait_ge(qkv_out, 2 * TT + m + 1)
                ins = nc.scalar.activation(qkv[:, :, 2, m * P:(m + 1) * P],
                                           bank(m).rearrange("p (a n) -> p a n", n=P), ACT.Copy)
                ins.then_inc((bank0_free, bank1_free, qkv_evac, qkv_evac)[m], 1)
            act.wait_ge(bank0_free, 1)
            act.wait_ge(bank1_free, 1)
            act.wait_ge(qkv_evac, 2 * TT + 2)

            def exponents(p, head):
                for n, i in enumerate(S_ORDER):
                    act.wait_ge(row_min, p * 8 + (4 * head + n + 1))
                    a, w = S_AT[i], P * (i + 1)
                    e = 4 * head + n
                    nc.scalar.activation(probs[:, a:a + w], probs[:, a:a + w], ACT.Exp, scale=-1.0,
                                         bias=rmin[:, e:e + 1], accum_out=psums[:, e:e + 1]).then_inc(exps, 1)

            def turn(p, last):
                act.wait_ge(qk_tr, p * 2 + 1)
                for head in range(2):
                    a, b = head * 64, head * 64 + 64
                    nc.scalar.activation(qs[a:b, head, :], bank(Q_BANK, p0=a, p1=b), ACT.Copy,
                                         scale=-(HEAD_DIM ** -0.5)).then_inc(qk_hi, 1)
                act.wait_ge(qk_tr, p * 2 + 2)
                for head in range(2):
                    a, b = head * 64, head * 64 + 64
                    for to in range(2):
                        nc.scalar.activation(k_hi[to * 64:to * 64 + 64, head, :], bank(K_BANK, p0=a, p1=b),
                                             ACT.Copy).then_inc(qk_hi, 1)
                for head in range(2):
                    hc = head * HEAD_DIM
                    src = qkv[:, p, 2, :] if last else qkv[:, bass.ds(p, 1), 2, :].rearrange("p a n -> p (a n)")
                    nc.scalar.activation(v2[:, head, :, hc:hc + HEAD_DIM],
                                         src.rearrange("p (m n) -> p m n", n=P)[:, :, hc:hc + HEAD_DIM],
                                         ACT.Copy).then_inc(v_hi, 1)
                for i in range(2):
                    act.wait_ge(qkv_out, 3 * TT)
                    act.wait_ge(raw_in[i], p * 16 + (16 * 6 + 16))
                    nc.scalar.activation(w_hi[:, bass.ds(p * 2 + i, 1)].rearrange("p a n -> p (a n)"),
                                         w_raw[:, i], ACT.Copy).then_inc(slab_hi, 1)
                if not last:
                    split_tile(CN, p * 32 + 32)
                exponents(p, 0)
                if not last:
                    split_tile(HN, p * 32 + 32)
                act.wait_ge(p_tr, p * 2 + 1)
                nc.scalar.activation(pt_hi[:, :], ps[:, TB:TB + TRI], ACT.Copy).then_inc(p_hi, 1)
                act.wait_ge(y_conv, p + 1)
                act.wait_ge(sq_added, p * 2 + 1)
                nc.scalar.activation(sq[:, :], yc[:, :], ACT.Square).then_inc(sq_ok, 1)
                exponents(p, 1)
                act.wait_ge(tile_out, p * NT + (ZC + 3))
                nc.scalar.activation(cz[:, :], bank(TILE_BANK[ZC]), ACT.Silu).then_inc(bank1_free, 1)
                if not last:
                    split_tile(B_, p * 32 + 48)
                act.wait_ge(qkv_evac, 2 * TT + 2)
                act.wait_ge(y_gated, p * 2 + 1)
                yp = y[:, p] if last else y[:, bass.ds(p, 1)].rearrange("p a s n -> p (a s) n")
                nc.scalar.activation(yp[:, 2], yg[:, :], ACT.Copy).then_inc(y_hi, 1)
                act.wait_ge(tile_out, p * NT + (ZA + 3))
                nc.scalar.activation(za[:, :], bank(TILE_BANK[ZA]), ACT.Silu).then_inc(bank0_free, 1)
                act.wait_ge(sq_added, p * 2 + 2)
                act.wait_ge(pv_out, p * 2 + 1)
                nc.scalar.activation(ytmp[0:64, :], bank(2, p0=64, p1=128), ACT.Copy).then_inc(y_tmp, 1)
                act.wait_ge(p_tr, p * 2 + 2)
                nc.scalar.activation(pt_hi[:, :], ps[:, TB:TB + TRI], ACT.Copy).then_inc(p_hi, 1)
                if not last:
                    split_tile(ZC, p * 32 + 48)
                if not last:
                    split_tile(ZA, p * 16 + 32)
                    act.wait_ge(tile_out, p * NT + (CN + 3))
                    nc.scalar.activation(cz[:, :], bank(C_BANK), ACT.Copy).then_inc(c_copy, 1)
                act.wait_ge(pv_out, p * 2 + 2)
                nc.scalar.activation(ytmp[64:128, :], bank(3, p0=0, p1=64), ACT.Copy).then_inc(y_tmp, 1)
                act.wait_ge(y_gated, p * 2 + 2)
                nc.scalar.activation(yp[:, 0], yg[:, :], ACT.Copy).then_inc(y_hi, 1)
                act.wait_ge(sq_added, p * 2 + 2)
                nc.scalar.activation(sq[:, :], ya[:, :], ACT.Square).then_inc(sq_ok, 1)

            with act.Fori(0, NP - 1) as p:
                turn(p, False)
            turn(NP - 1, True)

            act.wait_ge(conv_out, TT)
            for k in (4, 5, 6, 7):
                act.wait_ge(raw_in[k % 4], 16 * (7 + (4 if k % 4 < 2 else 0)))
                nc.scalar.activation(w_hi[:, k], w_raw[:, k % 4], ACT.Copy).then_inc(slab_hi, 1)
            act.wait_ge(rs_ok, 1)

            def square(e):
                n, m, lo, hi, _ = PIECES[e]
                act.wait_ge(x2_ok, e + 1)
                if e:
                    act.wait_ge(x2_sq, e)
                nc.scalar.activation(junk2[:, lo:hi], x2[:, m, n * BANK + lo:n * BANK + hi], ACT.Square,
                                     scale=D ** -0.5, accum_out=ss2[:, e:e + 1]).then_inc(x2_sq, 1)

            def scale_left(m):
                act.wait_ge(fin_rs, m + 1)
                nc.scalar.activation(x2[:, m, 0:BANK], x2[:, m, 0:BANK], ACT.Copy,
                                     scale=small[:, 56 + m:57 + m]).then_inc(fin_left, 1)

            for n in range(2):
                for m in range(TT):
                    if n:
                        act.wait_ge(attn_evac, m + 1)
                    act.wait_ge(conv_out, n * TT + m + 1)
                    nc.scalar.activation(oc[:, m], bank(CONV_BANK[m]), ACT.Copy, scale=rs[:, m:m + 1]
                                         ).then_inc(conv_evac, 1)
                if n == 0:
                    act.wait_ge(attn_out, TT)
                    for k in (0, 1, 2, 3):
                        act.wait_ge(raw_in[k % 4], 16 * (8 + (4 if k % 4 < 2 else 0)))
                        nc.scalar.activation(w_hi[:, k], w_raw[:, k % 4], ACT.Copy).then_inc(slab_hi, 1)
                    for e in range(TT):
                        square(e)
            for e in range(TT, len(PIECES)):
                square(e)
                if TT < e < 2 * TT:
                    scale_left(e - TT - 1)
            scale_left(TT - 1)

        @block.gpsimd
        def _(pool):
            nc.gpsimd.memset(ident[:, :], 0.0).then_inc(pool_step, 1)
            nc.gpsimd.memset(mask[:, :], 0.0).then_inc(pool_step, 1)
            nc.gpsimd.memset(small[:, 32:40], -0.5).then_inc(pool_step, 1)
            nc.gpsimd.memset(sqsum[:, :, :], 0.0).then_inc(sq_added, 1)
            pool.wait_ge(pool_step, 1)
            nc.gpsimd.affine_select(out=ident[:, :], in_=ident[:, :], compare_op=ALU.not_equal, fill=1.0, base=0,
                                    pattern=[[-1, P]], channel_multiplier=1).then_inc(ident_ok, 1)
            pool.wait_ge(pool_step, 2)
            nc.gpsimd.affine_select(out=mask[:, S - P:S], in_=mask[:, S - P:S], compare_op=ALU.is_ge, fill=MASKED,
                                    base=0, pattern=[[-1, P]], channel_multiplier=1).then_inc(mask_ok, 1)
            for m in range(TT):
                pool.wait_ge(x_sq, m + 1)
                nc.gpsimd.tensor_scalar(small[:, 8 + m:9 + m], small[:, m:m + 1], EPS, None, ALU.add
                                        ).then_inc(pool_step, 1)
                pool.wait_ge(pool_step, 4 + m)
                nc.gpsimd.tensor_tensor(small[:, 16 + m:17 + m], small[:, 8 + m:9 + m], small[:, 32:33], ALU.pow
                                        ).then_inc(x_rstd, 1)

            for j in range(KT):
                pool.wait_ge(slab_hi, j + 1)
                nc.gpsimd.tensor_tensor(ch_lo[:, j % 2], ch_raw[:, j % 4], ch_hi[:, j % 2].bitcast(F32), ALU.subtract)
                if 1 <= j < KT - 1:
                    pool.wait_ge(prods, 2 * j)
                    if j >= 2:
                        pool.wait_ge(chain, chained(j) + 1)
                    nc.gpsimd.tensor_tensor(prod_sum[:, :, :], prod[:, 0], prod[:, 1], ALU.add).then_inc(prods_added, 1)
                nc.gpsimd.tensor_tensor(w_lo[:, j], w_raw[:, j % 4], w_hi[:, j].bitcast(F32), ALU.subtract
                                        ).then_inc(slab_lo, 1)
                pool.wait_ge(hhi_ok, j + 1)
                nc.gpsimd.tensor_tensor(h_lo[:, j], h32[:, j % 2], h_hi[:, j].bitcast(F32), ALU.subtract
                                        ).then_inc(hlo_ok, 1)
            with pool.Fori(1, 3) as g:
                for k in range(KT):
                    pool.wait_ge(slab_hi, g * KT + (k + 1))
                    nc.gpsimd.tensor_tensor(w_lo[:, k], w_raw[:, k % 4], w_hi[:, k].bitcast(F32), ALU.subtract
                                            ).then_inc(slab_lo, 1)

            def split_tile(t, count):
                pool.wait_ge(tile_hi, count)
                nc.gpsimd.tensor_tensor(t_lo[:, t], tile_raw[:, RAW_SLOT[t]], t_hi[:, t].bitcast(F32), ALU.subtract
                                        ).then_inc(tile_lo, 1)

            for t in (B_, ZC, ZA):
                split_tile(t, t + 1)

            def turn(p, last):
                for head in range(2):
                    pool.wait_ge(v_hi, p * 2 + (head + 1))
                    hc, lc = head * HEAD_DIM, (1 - head) * HEAD_DIM
                    src = qkv[:, p, 2, :] if last else qkv[:, bass.ds(p, 1), 2, :].rearrange("p a n -> p (a n)")
                    nc.gpsimd.tensor_tensor(v2[:, head, :, lc:lc + HEAD_DIM],
                                            src.rearrange("p (m n) -> p m n", n=P)[:, :, hc:hc + HEAD_DIM],
                                            v2[:, head, :, hc:hc + HEAD_DIM].bitcast(F32), ALU.subtract
                                            ).then_inc(v_lo, 1)
                for i in range(2):
                    pool.wait_ge(slab_hi, p * 2 + (3 * KT + i + 1))
                    s = bass.ds(p * 2 + i, 1)
                    nc.gpsimd.tensor_tensor(w_lo[:, s].rearrange("p a n -> p (a n)"), w_raw[:, i],
                                            w_hi[:, s].rearrange("p a n -> p (a n)").bitcast(F32), ALU.subtract
                                            ).then_inc(slab_lo, 1)
                if not last:
                    split_tile(CN, p * NT + 4)
                    split_tile(HN, p * NT + 5)
                pool.wait_ge(sq_ok, p * 2 + 1)
                pool.wait_ge(sq_added, p * 2 + 1)
                nc.gpsimd.tensor_tensor(sqsum[:, 0], sqsum[:, 0], sq[:, :], ALU.add).then_inc(sq_added, 1)
                if not last:
                    split_tile(B_, p * NT + 6)
                yp = y[:, p] if last else y[:, bass.ds(p, 1)].rearrange("p a s n -> p (a s) n")
                pool.wait_ge(y_hi, p * 2 + 1)
                nc.gpsimd.tensor_tensor(yp[:, 3], yg[:, :], yp[:, 2].bitcast(F32), ALU.subtract).then_inc(y_lo, 1)
                if not last:
                    split_tile(ZC, p * NT + 7)
                if not last:
                    split_tile(ZA, p * NT + 8)
                pool.wait_ge(y_hi, p * 2 + 2)
                nc.gpsimd.tensor_tensor(yp[:, 1], yg[:, :], yp[:, 0].bitcast(F32), ALU.subtract).then_inc(y_lo, 1)
                pool.wait_ge(sq_ok, p * 2 + 2)
                nc.gpsimd.tensor_tensor(sqsum[:, 1], sqsum[:, 1], sq[:, :], ALU.add).then_inc(sq_added, 1)

            with pool.Fori(0, NP - 1) as p:
                turn(p, False)
            turn(NP - 1, True)
            pool.wait_ge(ssq_ok, 1)
            nc.gpsimd.tensor_tensor(rs[:, :], small[:, 40:48], small[:, 32:40], ALU.pow).then_inc(rs_ok, 1)
            pool.wait_ge(slab_hi, 4 * KT + 4)
            for k in (4, 5, 6, 7):
                nc.gpsimd.tensor_tensor(w_lo[:, k], w_raw[:, k % 4], w_hi[:, k].bitcast(F32), ALU.subtract
                                        ).then_inc(slab_lo, 1)
            for k in (0, 1, 2, 3):
                pool.wait_ge(slab_hi, 4 * KT + 4 + k + 1)
                nc.gpsimd.tensor_tensor(w_lo[:, k], w_raw[:, k % 4], w_hi[:, k].bitcast(F32), ALU.subtract
                                        ).then_inc(slab_lo, 1)
            pool.wait_ge(x2_sq, TT)
            nc.gpsimd.tensor_scalar(ss2[:, 0:TT], ss2[:, 0:TT], EPS, None, ALU.add).then_inc(ss2_eps, 1)
            pool.wait_ge(gfin_in, 16)
            for m in range(TT):
                nc.gpsimd.tensor_tensor(x2[:, m, 0:BANK], x2[:, m, 0:BANK], gfin[:, 0:BANK], ALU.mult).then_inc(x2_g, 1)
            pool.wait_ge(ss2_eps, 1)
            for m in range(TT):
                e = TT + m
                if m == TT - 1:
                    pool.wait_ge(x2_sq, e + 1)
                    nc.gpsimd.tensor_tensor(ss2[:, m:m + 1], ss2[:, m:m + 1], ss2[:, e:e + 1], ALU.add).then_inc(ss2_eps, 1)
                    pool.wait_ge(ss2_eps, 2)
                    e += 1
                pool.wait_ge(x2_g, m + 1)
                pool.wait_ge(x2_sq, e + 1)
                nc.gpsimd.tensor_scalar(small[:, 48 + m:49 + m], ss2[:, e:e + 1], ss2[:, m:m + 1], None,
                                        ALU.add).then_inc(pool_step, 1)
                pool.wait_ge(pool_step, 4 + TT + m)
                nc.gpsimd.tensor_tensor(small[:, 56 + m:57 + m], small[:, 48 + m:49 + m], small[:, 32:33], ALU.pow
                                        ).then_inc(fin_rs, 1)

        @block.vector
        def _(dve):
            steps = [0]

            def step(ins):
                ins.then_inc(dve_step, 1)
                steps[0] += 1
                dve.wait_ge(dve_step, steps[0])

            nc.vector.memset(ones[:, :], 1.0).then_inc(ones_ok, 1)
            nc.vector.memset(u[:, 0:CONV_TAPS - 1], 0.0).then_inc(ones_ok, 1)

            def sum_chunk(j, total):
                dve.wait_ge(ada_in[j % 3], 32 * (j // 3 + 1))
                shared = 1 < j < KT
                if shared:
                    dve.wait_ge(prods_added, j - 1)
                for r in range(RV if shared else R):
                    src = ada[:, j % 3, :, r, :]
                    if r == 0 and not shared:
                        ins = nc.vector.tensor_scalar(total, src, sc[:, 0:1], None, ALU.mult)
                    else:
                        if r:
                            dve.wait_ge(chain, chained(j) + r)
                        ins = nc.vector.scalar_tensor_tensor(out=total, in0=src, scalar=sc[:, r:r + 1],
                                                             in1=total if r else prod_sum[:, :, :],
                                                             op0=ALU.mult, op1=ALU.add)
                    ins.then_inc(chain, 1)
                    if KT - 3 <= j < KT:
                        angle_step(RV * (j - (KT - 3)) + r)

            def modulation(j):
                dve.wait_ge(mod_sum, j + 1)
                nc.vector.tensor_scalar(gs[:, j:j + 1], bank(7, 2 * j, 2 * j + 1), b1[:, j:j + 1], prmT[:, 24 + j:25 + j],
                                        ALU.add, ALU.mult).then_inc(mod_ok, 1)
                nc.vector.tensor_scalar(sh[:, j:j + 1], bank(7, 2 * j + 1, 2 * j + 2), prmT[:, j:j + 1], None,
                                        ALU.add).then_inc(mod_ok, 1)

            dve.wait_ge(pos_in, 32)
            nc.vector.tensor_copy(posf[0:TT, :], posi[0:TT, :]).then_inc(posf_ok, 1)
            dve.wait_ge(pos_tr, 1)
            nc.vector.tensor_copy(posT[:, :], bank(7, 128, 128 + TT)).then_inc(pos_read, 1)
            dve.wait_ge(pos_read, 1)
            for m in range(TT):
                ins = nc.vector.tensor_scalar(ang[:, m, :], invf[:, :], posT[:, m:m + 1], None, ALU.mult)
            ins.then_inc(angle, 1)
            pieces = two_pi_pieces(4, 2.0 ** -45)
            last_step = len(pieces) + 4
            assert last_step < 3 * RV

            def angle_step(i):
                if i > last_step:
                    return
                dve.wait_ge(angle, i + 1)
                if i == 0:
                    ins = nc.vector.tensor_scalar(turns[:, :, :], ang[:, :, :], TWO_PI_INV, ROUND, ALU.mult, ALU.add)
                elif i == 1:
                    ins = nc.vector.tensor_scalar(turns[:, :, :], turns[:, :, :], ROUND, None, ALU.subtract)
                elif i < last_step - 2:
                    ins = nc.vector.scalar_tensor_tensor(out=ang[:, :, :], in0=turns[:, :, :], scalar=-pieces[i - 2],
                                                         in1=ang[:, :, :], op0=ALU.mult, op1=ALU.add)
                elif i == last_step - 2:
                    ins = nc.vector.tensor_scalar(ang[:, :, :], ang[:, :, :], PI_BELOW, -PI_BELOW, ALU.min, ALU.max)
                elif i == last_step - 1:
                    ins = nc.vector.scalar_tensor_tensor(out=turns[:, :, :], in0=ang[:, :, :], scalar=-1.0,
                                                         in1=ang[:, :, :], op0=ALU.mult, op1=ALU.min)
                else:
                    ins = nc.vector.tensor_scalar(turns[:, :, :], turns[:, :, :], PI / 2, None, ALU.add)
                ins.then_inc(angle, 1)

            dve.wait_ge(silu_c, 1)
            sum_chunk(0, acc[:, 0])
            for m in range(TT):
                if m == TT - 1:
                    dve.wait_ge(prm_tr, 1)
                    step(nc.vector.tensor_copy(prmT[:, 0:52], bank(7, 64, 64 + 52)))
                    nc.vector.tensor_scalar(b1[:, :], prmT[:, 8:16], 1.0, None, ALU.add).then_inc(prm_ok, 1)
                dve.wait_ge(x_rstd, m + 1)
                nc.vector.tensor_scalar(xt[:, m, :], xt[:, m, :], small[:, 16 + m:17 + m], None,
                                        ALU.mult).then_inc(x_norm, 1)
            dve.wait_ge(prm_ok, 1)
            for j in range(KT):
                modulation(j)
                if j + 1 < KT:
                    if j + 1 >= 2:
                        dve.wait_ge(mod_sum, j)
                    sum_chunk(j + 1, acc[:, (j + 1) % 2])

            for i in range(GC):
                sum_chunk(KT + i, gate_acc[:, i].rearrange("p (a n) -> p a n", n=P))
            def rope_part(p, part, to, count):
                if isinstance(p, int):
                    raw = qkv[:, p, part, :]
                else:
                    raw = qkv[:, bass.ds(p, 1), part, :].rearrange("p a n -> p (a n)")
                raw = raw.rearrange("p (m h f) -> p m h f", h=2, f=HEAD_DIM)
                m1 = rope_m[:, 0].rearrange("p m (h f) -> p m h f", h=2)
                m2 = rope_m[:, 1].rearrange("p m (h f) -> p m h f", h=2)
                o = to.rearrange("p m (h f) -> p m h f", h=2)
                for h in range(2):
                    nc.vector.tensor_tensor(m1[:, :, h], raw[:, :, h], cos_t[:, :, :], ALU.mult)
                    ins = nc.vector.tensor_tensor(m2[:, :, h], raw[:, :, h], sin_t[:, :, :], ALU.mult)
                ins.then_inc(rope_ok, 1)
                dve.wait_ge(rope_ok, count)
                m1, m2 = (t.rearrange("p m (h f) -> p (m h) f", h=2) for t in (rope_m[:, 0], rope_m[:, 1]))
                o = to.rearrange("p m (h f) -> p (m h) f", h=2)
                nc.vector.tensor_tensor(o[:, :, 0:HALF], m1[:, :, 0:HALF], m2[:, :, HALF:], ALU.subtract)
                nc.vector.tensor_tensor(o[:, :, HALF:], m1[:, :, HALF:], m2[:, :, 0:HALF], ALU.add).then_inc(rope_ok, 1)

            def add_gate(i):
                dve.wait_ge(gate_sum, i + 1)
                gg = gate[:, i * 256:(i + 1) * 256]
                nc.vector.tensor_tensor(gg, gg, ps[:, 6 * BANK + i * 256:6 * BANK + (i + 1) * 256], ALU.add
                                        ).then_inc(gate_ok, 1)

            dve.wait_ge(trig_ok, 4)
            dve.wait_ge(qkv_evac, TT)
            rope_part(0, 0, rope_q, 1)
            dve.wait_ge(gate_in, 16)
            add_gate(0)
            add_gate(1)
            dve.wait_ge(rope_ok, 2)
            dve.wait_ge(qkv_evac, 2 * TT)
            rope_part(0, 1, rope_k, 3)
            add_gate(2)
            add_gate(3)

            def least(p, head):
                for n, i in enumerate(S_ORDER):
                    if n != 1:
                        count = p * 6 + (3 * head + max(n, 1))
                        if not isinstance(p, int):
                            dve.to_reg(count)
                        dve.wait_ge(mask_ok, 1)
                        dve.wait_ge(scores, count)
                    a, w = S_AT[i], P * (i + 1)
                    e = 4 * head + n
                    dve.tensor_tensor_reduce(probs[:, a:a + w], mask[:, S - w:S], ps[:, SB + a:SB + a + w], 1.0,
                                             3.0e38, ALU.add, ALU.min, rmin[:, e:e + 1]).then_inc(row_min, 1)

            def normalise(p, head, count):
                dve.wait_ge(exps, p * 8 + (4 * head + 4))
                nc.vector.reciprocal(prec[:, 4 * head:4 * head + 4], psums[:, 4 * head:4 * head + 4]).then_inc(p_norm, 1)
                dve.wait_ge(p_norm, p * 4 + (2 * head + 1))
                for n, i in enumerate(S_ORDER):
                    a, w = S_AT[i], P * (i + 1)
                    e = 4 * head + n
                    ins = nc.vector.tensor_scalar(probs[:, a:a + w], probs[:, a:a + w], prec[:, e:e + 1], None, ALU.mult)
                ins.then_inc(p_norm, 1)

            def low_probs(p, head):
                dve.wait_ge(p_hi, p * 2 + (head + 1))
                nc.vector.tensor_tensor(pt_lo[:, :], ps[:, TB:TB + TRI], pt_hi[:, :].bitcast(F32), ALU.subtract
                                        ).then_inc(p_lo, 1)

            dve.wait_ge(mask_ok, 1)

            def column(p, row, last):
                return prmT[:, row + p:row + p + 1] if last else prmT[:, bass.ds(p + row, 1)]

            def tap(p, i, last):
                wc = column(p, 40 + NP * i, last)
                if i == 0:
                    dve.wait_ge(u_ok, p + 1)
                    ins = nc.vector.tensor_scalar(yc[:, :], u[:, 0:S], wc, None, ALU.mult)
                else:
                    dve.wait_ge(tap_ok, p * 3 + i)
                    ins = nc.vector.scalar_tensor_tensor(out=yc[:, :], in0=u[:, i:i + S], scalar=wc, in1=yc[:, :],
                                                         op0=ALU.mult, op1=ALU.add)
                ins.then_inc(tap_ok, 1)

            def turn(p, last):
                dve.wait_ge(c_copy, p + 1)
                dve.wait_ge(tile_out, p * NT + 2)
                nc.vector.tensor_tensor(u[:, CONV_TAPS - 1:], cz[:, :], bank(H_BANK), ALU.mult).then_inc(u_ok, 1)
                dve.wait_ge(qk_hi, p * 6 + 2)
                for head in range(2):
                    a, b = head * 64, head * 64 + 64
                    o = (1 - head) * 64
                    nc.vector.scalar_tensor_tensor(out=qs[o:o + 64, head, :], in0=bank(Q_BANK, p0=a, p1=b),
                                                   scalar=-(HEAD_DIM ** -0.5), in1=qs[a:b, head, :].bitcast(F32),
                                                   op0=ALU.mult, op1=ALU.subtract)
                    if head == 0:
                        dve.wait_ge(qk_hi, p * 6 + 6)
                    for to in range(2):
                        ins = nc.vector.tensor_tensor(k_lo[to * 64:to * 64 + 64, head, :], bank(K_BANK, p0=a, p1=b),
                                                      k_hi[a:b, head, :].bitcast(F32), ALU.subtract)
                    ins.then_inc(qk_split, 1)
                tap(p, 0, last)
                least(p, 0)
                tap(p, 1, last)
                tap(p, 2, last)
                normalise(p, 0, 0)
                dve.wait_ge(tap_ok, p * 3 + 3)
                dve.wait_ge(tile_out, p * NT + (B_ + 3))
                nc.vector.tensor_tensor(yc[:, :], yc[:, :], bank(TILE_BANK[B_]), ALU.mult).then_inc(y_conv, 1)
                least(p, 1)
                low_probs(p, 0)
                normalise(p, 1, 0)
                dve.wait_ge(bank1_free, p + 2)
                dve.wait_ge(v_lo, p * 2 + 2)
                dve.wait_ge(y_conv, p + 1)
                nc.vector.scalar_tensor_tensor(out=yg[:, :], in0=yc[:, :], scalar=column(p, 36, last), in1=cz[:, :],
                                               op0=ALU.mult, op1=ALU.mult).then_inc(y_gated, 1)
                if not last:
                    rope_part(p + 1, 0, rope_q, p * 4 + 5)
                dve.wait_ge(y_tmp, p * 2 + 1)
                nc.vector.tensor_tensor(ya[0:64, :], ytmp[0:64, :], bank(2, p0=0, p1=64), ALU.add).then_inc(y_attn, 1)
                low_probs(p, 1)
                if not last:
                    dve.wait_ge(rope_ok, p * 4 + 6)
                    rope_part(p + 1, 1, rope_k, p * 4 + 7)
                dve.wait_ge(y_tmp, p * 2 + 2)
                nc.vector.tensor_tensor(ya[64:128, :], ytmp[64:128, :], bank(3, p0=64, p1=128), ALU.add
                                        ).then_inc(y_attn, 1)
                dve.wait_ge(bank0_free, p + 2)
                dve.wait_ge(y_lo, p * 2 + 1)
                dve.wait_ge(y_attn, p * 2 + 2)
                nc.vector.scalar_tensor_tensor(out=yg[:, :], in0=ya[:, :], scalar=column(p, 32, last), in1=za[:, :],
                                               op0=ALU.mult, op1=ALU.mult).then_inc(y_gated, 1)

            with dve.Fori(0, NP - 1) as p:
                turn(p, False)
            turn(NP - 1, True)

            dve.wait_ge(ssq_out, 1)
            nc.vector.tensor_scalar(small[:, 40:48], bank(7, 0, 8), 1.0 / DA, EPS, ALU.mult, ALU.add
                                    ).then_inc(ssq_ok, 1)
            dve.wait_ge(gate_ok, 4)
            dve.wait_ge(x2_in, 16 * TT)
            dve.wait_ge(rs_ok, 1)

            def add_conv(n, m):
                cols = slice(n * BANK, (n + 1) * BANK)
                dve.wait_ge(conv_evac, n * TT + m + 1)
                step(nc.vector.tensor_tensor(oc[:, m], oc[:, m], gate[:, cols], ALU.mult))
                nc.vector.tensor_tensor(x2[:, m, cols], x2[:, m, cols], oc[:, m], ALU.add).then_inc(conv_added, 1)

            def add_attn(e):
                n, m, lo, hi, b = PIECES[e]
                cols = slice(n * BANK + lo, n * BANK + hi)
                dve.wait_ge(attn_out, e + 1)
                nc.vector.scalar_tensor_tensor(out=om[:, e % 2, lo:hi], in0=bank(b, lo, hi), scalar=rs[:, TT + m:TT + m + 1],
                                               in1=gate[:, cols], op0=ALU.mult, op1=ALU.mult).then_inc(attn_evac, 1)
                dve.wait_ge(conv_added, n * TT + m + 1)
                dve.wait_ge(attn_evac, e + 1)
                nc.vector.tensor_tensor(x2[:, m, cols], x2[:, m, cols], om[:, e % 2, lo:hi], ALU.add).then_inc(x2_ok, 1)

            def scale_right(m):
                dve.wait_ge(fin_rs, m + 1)
                nc.vector.scalar_tensor_tensor(out=x2[:, m, BANK:], in0=x2[:, m, BANK:], scalar=small[:, 56 + m:57 + m],
                                               in1=gfin[:, BANK:], op0=ALU.mult, op1=ALU.mult).then_inc(fin_right, 1)

            for n in range(2):
                for m in range(TT):
                    add_conv(n, m)
                for e in range(TT * n, TT if n == 0 else len(PIECES)):
                    add_attn(e)
                    if e in (TT + 1, TT + 2):
                        scale_right(e - TT - 1)
            scale_right(TT - 2)
            scale_right(TT - 1)

        @block.tensor
        def _(pe):
            def mm3(o, a_hi, a_lo, b_hi, b_lo, start, stop):
                nc.tensor.matmul(o, a_hi, b_lo, start=start, stop=False)
                nc.tensor.matmul(o, a_lo, b_hi, start=False, stop=False)
                return nc.tensor.matmul(o, a_hi, b_hi, start=False, stop=stop)

            pe.wait_ge(ident_ok, 1)
            pe.wait_ge(posf_ok, 1)
            nc.tensor.transpose(bank(7, 128, 128 + TT), posf[0:TT, :], ident[0:TT, 0:TT]).then_inc(pos_tr, 1)
            pe.wait_ge(ones_ok, 1)

            def x_tile(j):
                if j:
                    pe.wait_ge(h_ok, j)
                for m in range(TT):
                    if j == 0:
                        if m == TT - 1:
                            keep_busy(1)
                        pe.wait_ge(x_norm, m + 1)
                    ins = nc.tensor.transpose(bank(6, m * P, (m + 1) * P), xt[:, m, j * P:(j + 1) * P], ident[:, :])
                ins.then_inc(x_tr, 1)

            def mod_tile(j):
                pe.wait_ge(chain, chained(j + 1))
                for two in range(2):
                    ins = nc.tensor.matmul(bank(7, 2 * j + two, 2 * j + two + 1), acc[:, j % 2, two, :], ones[:, 0:1],
                                           start=True, stop=True)
                ins.then_inc(mod_sum, 1)

            def keep_busy(n):
                pe.wait_ge(slab_hi, 1)
                for _ in range(n):
                    nc.tensor.matmul(bank(C_BANK), ch_hi[:, 0, 0], w_hi[:, 0, :], start=True, stop=True)

            def first_products():
                pe.wait_ge(slab_hi, 1)
                pe.wait_ge(hhi_ok, 1)
                for two, b in ((0, C_BANK), (1, H_BANK)):
                    nc.tensor.matmul(bank(b), ch_hi[:, 0, two], h_hi[:, 0], start=True, stop=False)
                for m in range(TT):
                    nc.tensor.matmul(bank(m), h_hi[:, 0, m * P:(m + 1) * P], w_hi[:, 0, :], start=True, stop=False)

            def mm2(o, a_hi, a_lo, b_hi, b_lo):
                nc.tensor.matmul(o, a_hi, b_lo, start=False, stop=False)
                return nc.tensor.matmul(o, a_lo, b_hi, start=False, stop=False)

            def slab(g, k):
                for m in range(TT):
                    if not isinstance(g, int) and k == 0:
                        pe.wait_ge(qkv_evac, g * TT + (m + 1 - TT))
                    t = slice(m * P, (m + 1) * P)
                    operands = bank(m), h_hi[:, k, t], h_lo[:, k, t], w_hi[:, k, :], w_lo[:, k, :]
                    if isinstance(g, int) and k == 0:
                        ins = mm2(*operands)
                    else:
                        ins = mm3(*operands, k == 0, k == KT - 1)
                    if k == KT - 1:
                        ins.then_inc(qkv_out, 1)
                if k < KT - 1:
                    ins.then_inc(slab_used, 1)

            pe.wait_ge(pos_read, 1)
            mod_tile(0)
            pe.wait_ge(prm_in, 16 * 5)
            nc.tensor.transpose(bank(7, 64, 64 + 52), prm[0:52, :], ident[0:52, 0:52]).then_inc(prm_tr, 1)
            x_tile(0)
            keep_busy(4)
            first_products()
            x_tile(1)
            mod_tile(1)
            for j in range(KT):
                if 1 < j < KT - 1:
                    mod_tile(j + 1)
                pe.wait_ge(slab_lo, j + 1)
                pe.wait_ge(hlo_ok, j + 1)
                for two, b in ((0, C_BANK), (1, H_BANK)):
                    operands = bank(b), ch_hi[:, j % 2, two], ch_lo[:, j % 2, two], h_hi[:, j], h_lo[:, j]
                    ins = mm3(*operands, False, j == KT - 1) if j else mm2(*operands)
                    if j == KT - 1:
                        ins.then_inc(tile_out, 1)
                if j < KT - 1:
                    ins.then_inc(ch_used, 1)
                if j == 1:
                    mod_tile(2)
                slab(0, j)
                if j + 2 < KT:
                    x_tile(j + 2)

            with pe.Fori(1, 3) as g:
                for k in range(KT):
                    pe.wait_ge(slab_lo, g * KT + (k + 1))
                    slab(g, k)
                    if k in (KT - 3, KT - 2):
                        i = k - (KT - 3)
                        pe.wait_ge(chain, g * (2 * R) + (chained(KT) - 2 * R + (i + 1) * R))
                        if i:
                            pe.wait_ge(gate_ok, g * 2 - 1)
                        nc.tensor.matmul(ps[:, bass.ds(g * 512 + (6 * BANK - 512 + i * 256), 256)], ones[:, :],
                                         gate_acc[:, bass.ds(g * 2 + (i - 2), 1)].rearrange("p a n -> p (a n)"),
                                         start=True, stop=True).then_inc(gate_sum, 1)

            BANK_FREE = [bank0_free, bank1_free, y_conv, None, None]

            def tile(p, t):
                pe.wait_ge(tile_lo, p * NT + (t + 1))
                if BANK_FREE[t]:
                    pe.wait_ge(BANK_FREE[t], p + 1)
                for k in range(KT):
                    ins = mm3(bank(TILE_BANK[t]), t_hi[:, t, k], t_lo[:, t, k], h_hi[:, k], h_lo[:, k],
                              k == 0, k == KT - 1)
                ins.then_inc(tile_out, 1)

            def score(p, head):
                for n, i in enumerate(S_ORDER):
                    o = ps[:, SB + S_AT[i]:SB + S_AT[i] + P * (i + 1)]
                    q = qs[:, head, i * P:(i + 1) * P]
                    nc.tensor.matmul(o, q, k_lo[:, head, 0:P * (i + 1)], start=True, stop=False)
                    ins = nc.tensor.matmul(o, q, k_hi[:, head, 0:P * (i + 1)], start=False, stop=True)
                    if n:
                        ins.then_inc(scores, 1)

            def transpose_probs():
                for i in range(TT):
                    for j in range(i + 1):
                        a = S_AT[i] + j * P
                        o = TB + T_AT[j] + (i - j) * P
                        ins = nc.tensor.transpose(ps[:, o:o + P], probs[:, a:a + P], ident[:, :])
                ins.then_inc(p_tr, 1)

            def values(head):
                for j in range(TT):
                    for n, pt in enumerate((pt_lo, pt_hi)):
                        ins = nc.tensor.matmul(bank(2 + head, j * P, BANK), v2[:, head, j, :],
                                               pt[:, T_AT[j]:T_AT[j] + S - j * P],
                                               start=(j == 0 and n == 0), stop=(j == TT - 1 and n == 1))
                ins.then_inc(pv_out, 1)

            def project(part, m, b, rows, lo=0, hi=BANK):
                t = slice(m * P, (m + 1) * P)
                for k in range(NP):
                    ins = mm3(bank(b, lo, hi), y[:, k, part, t], y[:, k, part + 1, t], w_hi[:, rows + k, lo:hi],
                              w_lo[:, rows + k, lo:hi], k == 0, k == NP - 1)
                return ins

            def turn(p, last):
                for n, (src, b) in enumerate(((rope_q, Q_BANK), (rope_k, K_BANK))):
                    pe.wait_ge(rope_ok, p * 4 + (2 * n + 2))
                    if n == 0:
                        pe.wait_ge(gate_ok, GC)
                    for m in range(TT):
                        ins = nc.tensor.transpose(bank(b, m * P, (m + 1) * P), src[:, m, :], ident[:, :])
                    ins.then_inc(qk_tr, 1)
                tile(p, B_)
                pe.wait_ge(qk_split, p * 2 + 1)
                score(p, 0)
                tile(p, ZC)
                pe.wait_ge(p_norm, p * 4 + 2)
                transpose_probs()
                pe.wait_ge(qk_split, p * 2 + 2)
                score(p, 1)
                tile(p, ZA)
                pe.wait_ge(p_lo, p * 2 + 1)
                pe.wait_ge(v_lo, p * 2 + 2)
                pe.wait_ge(row_min, p * 8 + 8)
                values(0)
                pe.wait_ge(p_norm, p * 4 + 4)
                transpose_probs()
                if last:
                    pe.wait_ge(slab_lo, 4 * KT)
                    pe.wait_ge(y_lo, 2 * NP - 1)
                    pe.wait_ge(bank1_free, NP + 1)
                    for m in range(2):
                        project(2, m, CONV_BANK[m], NP).then_inc(conv_out, 1)
                else:
                    tile(p, CN)
                pe.wait_ge(p_lo, p * 2 + 2)
                values(1)
                if not last:
                    tile(p, HN)

            with pe.Fori(0, NP - 1) as p:
                turn(p, False)
            turn(NP - 1, True)

            pe.wait_ge(bank0_free, NP + 1)
            pe.wait_ge(y_attn, 2 * NP - 1)
            for m in (2, 3):
                project(2, m, CONV_BANK[m], NP).then_inc(conv_out, 1)
            pe.wait_ge(y_attn, 2 * NP)
            pe.wait_ge(y_lo, 2 * NP)
            for m in range(TT):
                if m == 1:
                    pe.wait_ge(sq_added, 2 * NP + 1)
                    for part in range(2):
                        for i in range(TT):
                            ins = nc.tensor.matmul(bank(7, part * TT + i, part * TT + i + 1),
                                                   sqsum[:, part, i * P:(i + 1) * P], ones[:, 0:1], start=True, stop=True)
                    ins.then_inc(ssq_out, 1)
                if m == 3:
                    pe.wait_ge(ssq_ok, 1)
                project(0, m, ATTN_BANK[m], 0).then_inc(attn_out, 1)
            pe.wait_ge(slab_lo, 4 * KT + 4)
            for m in range(TT):
                pe.wait_ge(conv_evac, m + 1)
                project(2, m, CONV_BANK[m], NP).then_inc(conv_out, 1)
            pe.wait_ge(slab_lo, 5 * KT)
            for n, m, lo, hi, b in PIECES[TT:]:
                pe.wait_ge(attn_evac, m + 1)
                pe.wait_ge(conv_evac, TT + 1)
                project(0, m, b, 0, lo, hi).then_inc(attn_out, 1)


_INS = ["x", "c", "positions", "w_ada", "b_ada", "g_norm", "w_in", "w_conv", "g_attn_out", "g_conv_out",
        "w_out", "g_final"]


def kernel(**inputs):
    import numpy as np
    import concourse.bacc as bacc
    from concourse.bass_utils import run_bass_kernel_spmd as run

    nc = bacc.Bacc("TRN2", target_bir_lowering=False, num_devices=1, dynamic_dma_scratch_size=64)
    arrays, args = {}, []
    given = [(name, np.ascontiguousarray(inputs[name])) for name in _INS]
    half = HEAD_DIM // 2
    given.append(("inv_freq", (10000.0 ** (-np.arange(half) / half)).astype(np.float32)))
    for name, a in given:
        arrays[f"in_{name}"] = a
        args.append(nc.dram_tensor(f"in_{name}", a.shape, mybir.dt.from_np(a.dtype), kind="ExternalInput").ap())
    shape = inputs["x"].shape
    args.append(nc.dram_tensor("out_0", shape, F32, kind="ExternalOutput").ap())
    build(nc, *args)
    r = run(nc, [arrays], core_ids=[0])
    return r.results[0]["out_0"]
```
